# Optimizing a Trainium2 kernel written in Bass

```python
import numpy as np
import jax
import jax.numpy as jnp
from jax import lax

D_MODEL = 1024
BATCH = 1
SEQ = 256
DEPTH = 1

HEAD_DIM = 64
ROPE_THETA = 500000.0
LN_EPS = 1e-5

NSA_HEADS = 8
NSA_KV_HEADS = 2
CMP_LEN = 32
CMP_STRIDE = 16
CMP_HIDDEN = 128
SEL_BLOCK = 64
SEL_COUNT = 16
WINDOW = 512
NSA_Q_CHUNK = 64
FORCE_BONUS = 1e4

DSA_HEADS = 4
IDX_HEADS = 8
IDX_DIM = 32
DSA_TOPK_MAX = 256
DSA_Q_CHUNK = 128

MEM_HEADS = 4
MEM_LEN = 256

PEER_HEADS = 8
PEER_N_KEYS = 128
PEER_KEY_DIM = 256
PEER_TOPK = 16
PEER_CHUNK = 128
PEER_N_EXPERTS = PEER_N_KEYS * PEER_N_KEYS

DEEPNORM_ALPHA = (2.0 * DEPTH) ** 0.25
DEEPNORM_BETA = (8.0 * DEPTH) ** -0.25

IN_SPLITS = (
    NSA_HEADS * HEAD_DIM,
    6 * NSA_KV_HEADS * HEAD_DIM,
    3 * NSA_HEADS,
    DSA_HEADS * HEAD_DIM,
    2 * HEAD_DIM,
    IDX_HEADS * IDX_DIM,
    IDX_DIM,
    IDX_HEADS,
    MEM_HEADS * HEAD_DIM,
)
IN_WIDTH = sum(IN_SPLITS)

kernel_name = 'hybrid_nsa_dsa_mem_peer_deepnorm'

def layer_norm(x, g, b):
    xf = x.astype(jnp.float32)
    mu = jnp.mean(xf, axis=-1, keepdims=True)
    var = jnp.mean(jnp.square(xf - mu), axis=-1, keepdims=True)
    return ((xf - mu) * lax.rsqrt(var + LN_EPS) * g + b).astype(x.dtype)

def rope_partial(x, pos):
    r = x.shape[-1] // 4
    half = r // 2
    freqs = jnp.power(ROPE_THETA, -jnp.arange(half, dtype=jnp.float32) * 2.0 / r)
    ang = pos.astype(jnp.float32)[..., None] * freqs
    cos = jnp.cos(ang)[:, :, None, :]
    sin = jnp.sin(ang)[:, :, None, :]
    xf = x.astype(jnp.float32)
    x1 = xf[..., :half]
    x2 = xf[..., half:r]
    out = jnp.concatenate([x1 * cos - x2 * sin, x2 * cos + x1 * sin, xf[..., r:]], axis=-1)
    return out.astype(x.dtype)

def masked_softmax(s, mask):
    s = jnp.where(mask, s.astype(jnp.float32), -jnp.inf)
    m = jnp.max(s, axis=-1, keepdims=True)
    m = jnp.where(jnp.isfinite(m), m, 0.0)
    e = jnp.exp(s - m)
    den = jnp.sum(e, axis=-1, keepdims=True)
    return e / jnp.where(den > 0, den, 1.0)

def compress_blocks(kv, pe, w1, w2):
    B, S, G, d = kv.shape
    nc = (S - CMP_LEN) // CMP_STRIDE + 1
    idx = jnp.arange(nc)[:, None] * CMP_STRIDE + jnp.arange(CMP_LEN)[None, :]
    blocks = kv[:, idx] + pe[:, None, :]
    flat = blocks.transpose(0, 1, 3, 2, 4).reshape(B, nc, G, CMP_LEN * d)
    return jax.nn.gelu(flat @ w1, approximate=False) @ w2

def nsa_attention(q, kc, vc, ks, vs, kw, vw, gates):
    B, S, H, d = q.shape
    G = ks.shape[2]
    hpg = H // G
    C = NSA_Q_CHUNK
    scale = d ** -0.5
    nc = kc.shape[1]
    n_blocks = S // SEL_BLOCK
    n_pick = min(SEL_COUNT, n_blocks)
    qg = q.reshape(B, S, G, hpg, d).transpose(0, 2, 3, 1, 4)
    gg = gates.reshape(B, S, G, hpg, 3).transpose(0, 2, 3, 1, 4)
    kc = kc.transpose(0, 2, 1, 3)
    vc = vc.transpose(0, 2, 1, 3)
    ks_b = ks.transpose(0, 2, 1, 3).reshape(B, G, n_blocks, SEL_BLOCK, d)
    vs_b = vs.transpose(0, 2, 1, 3).reshape(B, G, n_blocks, SEL_BLOCK, d)
    pad = ((0, 0), (0, 0), (WINDOW, 0), (0, 0))
    kw_p = jnp.pad(kw.transpose(0, 2, 1, 3), pad)
    vw_p = jnp.pad(vw.transpose(0, 2, 1, 3), pad)
    c_start = jnp.arange(nc) * CMP_STRIDE
    cmp_end = c_start + CMP_LEN - 1
    blk_ids = jnp.arange(n_blocks)
    s_start = blk_ids * SEL_BLOCK
    overlap = jnp.clip(jnp.minimum(c_start[:, None] + CMP_LEN, s_start[None, :] + SEL_BLOCK)
                       - jnp.maximum(c_start[:, None], s_start[None, :]), 0).astype(jnp.float32) / CMP_LEN
    in_blk = jnp.arange(SEL_BLOCK)
    b_ix = jnp.arange(B)[:, None, None, None]
    g_ix = jnp.arange(G)[None, :, None, None]

    def chunk(c):
        t0 = c * C
        t = t0 + jnp.arange(C)
        qc = lax.dynamic_slice_in_dim(qg, t0, C, axis=3)
        gc = lax.dynamic_slice_in_dim(gg, t0, C, axis=3)
        s_cmp = jnp.einsum('bghcd,bgnd->bghcn', qc, kc) * scale
        p_cmp = masked_softmax(s_cmp, cmp_end[None, :] <= t[:, None])
        o_cmp = jnp.einsum('bghcn,bgnd->bghcd', p_cmp, vc)
        imp = jnp.einsum('bghcn,nm->bgcm', p_cmp, overlap)
        cur = t // SEL_BLOCK
        forced = (blk_ids[None, :] == 0) | (blk_ids[None, :] == cur[:, None]) | (blk_ids[None, :] == cur[:, None] - 1)
        visible = s_start[None, :] <= t[:, None]
        sel_score = jnp.where(visible, imp + FORCE_BONUS * forced, -jnp.inf)
        _, sel = lax.top_k(sel_score, n_pick)
        k_sel = ks_b[b_ix, g_ix, sel].reshape(B, G, C, n_pick * SEL_BLOCK, d)
        v_sel = vs_b[b_ix, g_ix, sel].reshape(B, G, C, n_pick * SEL_BLOCK, d)
        pos_sel = (sel[..., None] * SEL_BLOCK + in_blk).reshape(B, G, C, n_pick * SEL_BLOCK)
        s_sel = jnp.einsum('bghcd,bgckd->bghck', qc, k_sel) * scale
        p_sel = masked_softmax(s_sel, (pos_sel <= t[:, None])[:, :, None])
        o_sel = jnp.einsum('bghck,bgckd->bghcd', p_sel, v_sel)
        kwc = lax.dynamic_slice_in_dim(kw_p, t0, WINDOW + C, axis=2)
        vwc = lax.dynamic_slice_in_dim(vw_p, t0, WINDOW + C, axis=2)
        pos_w = t0 - WINDOW + jnp.arange(WINDOW + C)
        win_mask = (pos_w[None, :] <= t[:, None]) & (pos_w[None, :] > t[:, None] - WINDOW) & (pos_w[None, :] >= 0)
        s_win = jnp.einsum('bghcd,bgkd->bghck', qc, kwc) * scale
        p_win = masked_softmax(s_win, win_mask)
        o_win = jnp.einsum('bghck,bgkd->bghcd', p_win, vwc)
        return gc[..., 0:1] * o_cmp + gc[..., 1:2] * o_sel + gc[..., 2:3] * o_win

    out = lax.map(chunk, jnp.arange(S // C))
    return out.transpose(1, 0, 4, 2, 3, 5).reshape(B, S, H * d)

def dsa_attention(q, k, v, q_idx, k_idx, w_idx):
    B, S, H, d = q.shape
    C = DSA_Q_CHUNK
    topk = min(DSA_TOPK_MAX, S // 4)
    scale = d ** -0.5
    w = w_idx * (IDX_HEADS ** -0.5 * IDX_DIM ** -0.5)
    key_pos = jnp.arange(S)
    b_ix = jnp.arange(B)[:, None, None]

    def chunk(c):
        t0 = c * C
        t = t0 + jnp.arange(C)
        qi = lax.dynamic_slice_in_dim(q_idx, t0, C, axis=1)
        wi = lax.dynamic_slice_in_dim(w, t0, C, axis=1)
        logits = jax.nn.relu(jnp.einsum('bchd,bsd->bchs', qi, k_idx))
        score = jnp.einsum('bchs,bch->bcs', logits, wi).astype(jnp.float32)
        score = jnp.where(key_pos[None, :] <= t[:, None], score, -jnp.inf)
        _, sel = lax.top_k(score, topk)
        k_sel = k[b_ix, sel]
        v_sel = v[b_ix, sel]
        qc = lax.dynamic_slice_in_dim(q, t0, C, axis=1)
        s = jnp.einsum('bchd,bckd->bchk', qc, k_sel) * scale
        p = masked_softmax(s, (sel <= t[:, None])[:, :, None, :])
        return jnp.einsum('bchk,bckd->bchd', p, v_sel)

    out = lax.map(chunk, jnp.arange(S // C))
    return out.transpose(1, 0, 2, 3, 4).reshape(B, S, H * d)

def memory_attention(q, mem_k, mem_v):
    B, S, H, d = q.shape
    s = jnp.einsum('bshd,bmhd->bhsm', q, mem_k) * (d ** -0.5)
    p = jax.nn.softmax(s.astype(jnp.float32), axis=-1)
    return jnp.einsum('bhsm,bmhd->bshd', p, mem_v).reshape(B, S, H * d)

def peer(x, w_query, sub_keys_1, sub_keys_2, expert_u, expert_v):
    B, S, D = x.shape
    T = B * S
    half = PEER_KEY_DIM // 2
    xt = x.reshape(T, D)
    qh = (xt @ w_query).reshape(T, PEER_HEADS, PEER_KEY_DIM)
    s1 = jnp.einsum('thd,nd->thn', qh[..., :half], sub_keys_1)
    s2 = jnp.einsum('thd,nd->thn', qh[..., half:], sub_keys_2)
    v1, i1 = lax.top_k(s1, PEER_TOPK)
    v2, i2 = lax.top_k(s2, PEER_TOPK)
    cand = (v1[..., :, None] + v2[..., None, :]).reshape(T, PEER_HEADS, PEER_TOPK * PEER_TOPK)
    cand_idx = (i1[..., :, None] * PEER_N_KEYS + i2[..., None, :]).reshape(T, PEER_HEADS, PEER_TOPK * PEER_TOPK)
    top_s, top_j = lax.top_k(cand, PEER_TOPK)
    experts = jnp.take_along_axis(cand_idx, top_j, axis=-1).reshape(T, PEER_HEADS * PEER_TOPK)
    gate = jax.nn.softmax(top_s.astype(jnp.float32), axis=-1).reshape(T, PEER_HEADS * PEER_TOPK)
    C = PEER_CHUNK

    def chunk(c):
        t0 = c * C
        xc = lax.dynamic_slice_in_dim(xt, t0, C, axis=0)
        ec = lax.dynamic_slice_in_dim(experts, t0, C, axis=0)
        gc = lax.dynamic_slice_in_dim(gate, t0, C, axis=0)
        u = expert_u[ec]
        a = jax.nn.gelu(jnp.einsum('cd,ced->ce', xc, u).astype(jnp.float32), approximate=False)
        return jnp.einsum('ce,ced->cd', (gc * a).astype(x.dtype), expert_v[ec])

    y = lax.map(chunk, jnp.arange(T // C))
    return y.reshape(B, S, D)

def setup_inputs(seed: int = 0) -> dict:
    key = jax.random.key(seed)
    ks = jax.random.split(key, 24)
    f32 = jnp.float32
    d = HEAD_DIM
    nrm = lambda k, shape, s: jax.random.normal(k, shape, f32) * s
    x = nrm(ks[0], (BATCH, SEQ, D_MODEL), 1.0)
    mem = nrm(ks[1], (BATCH, MEM_LEN, D_MODEL), 1.0)
    start = jax.random.randint(ks[2], (BATCH, 1), 0, 2048)
    positions = (start + jnp.arange(SEQ)[None, :]).astype(jnp.int32)
    half = PEER_KEY_DIM // 2
    return {
        'x': x,
        'mem': mem,
        'positions': positions,
        'w_in': nrm(ks[3], (DEPTH, D_MODEL, IN_WIDTH), D_MODEL ** -0.5),
        'nsa_pe_k': nrm(ks[4], (DEPTH, CMP_LEN, d), 0.1),
        'nsa_pe_v': nrm(ks[5], (DEPTH, CMP_LEN, d), 0.1),
        'nsa_cmp_w1_k': nrm(ks[6], (DEPTH, CMP_LEN * d, CMP_HIDDEN), (CMP_LEN * d) ** -0.5),
        'nsa_cmp_w2_k': nrm(ks[7], (DEPTH, CMP_HIDDEN, d), CMP_HIDDEN ** -0.5),
        'nsa_cmp_w1_v': nrm(ks[8], (DEPTH, CMP_LEN * d, CMP_HIDDEN), (CMP_LEN * d) ** -0.5),
        'nsa_cmp_w2_v': nrm(ks[9], (DEPTH, CMP_HIDDEN, d), CMP_HIDDEN ** -0.5),
        'w_mem_kv': nrm(ks[10], (DEPTH, D_MODEL, 2 * MEM_HEADS * d), D_MODEL ** -0.5),
        'w_out': nrm(ks[11], (DEPTH, D_MODEL, D_MODEL), D_MODEL ** -0.5 * DEEPNORM_BETA),
        'ln1_g': 1.0 + nrm(ks[12], (DEPTH, D_MODEL), 0.02),
        'ln1_b': nrm(ks[13], (DEPTH, D_MODEL), 0.02),
        'peer_w_query': nrm(ks[14], (DEPTH, D_MODEL, PEER_HEADS * PEER_KEY_DIM), D_MODEL ** -0.5),
        'peer_sub_keys_1': nrm(ks[15], (DEPTH, PEER_N_KEYS, half), half ** -0.5),
        'peer_sub_keys_2': nrm(ks[16], (DEPTH, PEER_N_KEYS, half), half ** -0.5),
        'peer_u': nrm(ks[17], (DEPTH, PEER_N_EXPERTS, D_MODEL), D_MODEL ** -0.5),
        'peer_v': nrm(ks[18], (DEPTH, PEER_N_EXPERTS, D_MODEL), DEEPNORM_BETA),
        'ln2_g': 1.0 + nrm(ks[19], (DEPTH, D_MODEL), 0.02),
        'ln2_b': nrm(ks[20], (DEPTH, D_MODEL), 0.02),
    }

def reference(x, mem, positions, w_in, nsa_pe_k, nsa_pe_v, nsa_cmp_w1_k, nsa_cmp_w2_k,
              nsa_cmp_w1_v, nsa_cmp_w2_v, w_mem_kv, w_out, ln1_g, ln1_b, peer_w_query,
              peer_sub_keys_1, peer_sub_keys_2, peer_u, peer_v, ln2_g, ln2_b):
    B, S, _ = x.shape
    M = mem.shape[1]
    d = HEAD_DIM
    G = NSA_KV_HEADS
    split_points = np.cumsum(IN_SPLITS)[:-1].tolist()
    for layer in range(DEPTH):
        h = x @ w_in[layer]
        nsa_q, nsa_kv, nsa_gate, dsa_q, dsa_kv, idx_q, idx_k, idx_w, mem_q = jnp.split(h, split_points, axis=-1)
        q_n = rope_partial(nsa_q.reshape(B, S, NSA_HEADS, d), positions)
        kv_n = nsa_kv.reshape(B, S, 6, G, d)
        kc = compress_blocks(rope_partial(kv_n[:, :, 0], positions), nsa_pe_k[layer],
                             nsa_cmp_w1_k[layer], nsa_cmp_w2_k[layer])
        vc = compress_blocks(kv_n[:, :, 1], nsa_pe_v[layer], nsa_cmp_w1_v[layer], nsa_cmp_w2_v[layer])
        k_slc = rope_partial(kv_n[:, :, 2], positions)
        k_win = rope_partial(kv_n[:, :, 4], positions)
        gates = jax.nn.sigmoid(nsa_gate.reshape(B, S, NSA_HEADS, 3).astype(jnp.float32))
        o_nsa = nsa_attention(q_n, kc, vc, k_slc, kv_n[:, :, 3], k_win, kv_n[:, :, 5], gates)
        q_d = rope_partial(dsa_q.reshape(B, S, DSA_HEADS, d), positions)
        k_d = rope_partial(dsa_kv[..., :d][:, :, None, :], positions)[:, :, 0]
        v_d = dsa_kv[..., d:]
        qi = rope_partial(idx_q.reshape(B, S, IDX_HEADS, IDX_DIM), positions)
        ki = rope_partial(idx_k[:, :, None, :], positions)[:, :, 0]
        o_dsa = dsa_attention(q_d, k_d, v_d, qi, ki, idx_w)
        mkv = (mem @ w_mem_kv[layer]).reshape(B, M, 2, MEM_HEADS, d)
        o_mem = memory_attention(mem_q.reshape(B, S, MEM_HEADS, d), mkv[:, :, 0], mkv[:, :, 1])
        mix = jnp.concatenate([o_nsa, o_dsa, o_mem], axis=-1).astype(x.dtype) @ w_out[layer]
        x = layer_norm(DEEPNORM_ALPHA * x + mix, ln1_g[layer], ln1_b[layer])
        y = peer(x, peer_w_query[layer], peer_sub_keys_1[layer], peer_sub_keys_2[layer],
                 peer_u[layer], peer_v[layer])
        x = layer_norm(DEEPNORM_ALPHA * x + y, ln2_g[layer], ln2_b[layer])
    return x


_drawn_inputs = setup_inputs


def setup_inputs(seed=0):
    import zlib

    import numpy as np

    out = dict(_drawn_inputs(seed))
    spreads = {}
    factors = {'nsa_pe_k': 6.483, 'ln2_g': 2.842, 'ln2_b': 2.949}
    for name, (base, spread) in spreads.items():
        noise = np.random.default_rng([zlib.crc32(name.encode()), seed]).standard_normal(out[name].shape)
        drawn = base * np.exp(spread * noise) if base else spread * noise
        out[name] = jnp.asarray(drawn.astype(out[name].dtype))
    for name, factor in factors.items():
        out[name] = (out[name] * factor).astype(out[name].dtype)
    return out
```

```python
from contextlib import ExitStack

import numpy as np
import concourse.bass as bass
import concourse.mybir as mybir

F32 = mybir.dt.float32
F32R = mybir.dt.float32r
I32 = mybir.dt.int32
U32 = mybir.dt.uint32
ALU = mybir.AluOpType
ACT = mybir.ActivationFunctionType
AX_X = mybir.AxisListType.X

P = 128
D = 1024
S = 256
T = S // P
KD = D // P
HD = 64
SCALE = HD ** -0.5
CMP_LEN, CMP_STRIDE = 32, 16
NC = (S - CMP_LEN) // CMP_STRIDE + 1
LP = CMP_LEN * HD // P
MEM = 256
TOPK_DSA = min(256, S // 4)
IDX_H, IDX_D = 8, 32
PH = 8
NK = 128
TK = 16
ALPHA = 2.0 ** 0.25
EPS = 1e-5
NEG = -1e38
TAKEN = -3e38
TWO_PI = (6.28125, 0.0019350051879882812, 2 * np.pi - 6.28125 - 0.0019350051879882812)
PI_IN = 3.1415925
POOL_HOT = 2
RB = 4
MAGIC = 1.5 * 2 ** 23

C_NQ, C_KC, C_KS, C_KW, C_DQ, C_KD = 0, 512, 640, 768, 896, 1152
C_IQ, C_IK = 1216, 1472
C_VC, C_VS, C_VW, C_VD, C_GATE, C_IW = 1504, 1632, 1760, 1888, 1952, 1976
C_ALL = 1984
N64 = 19
N32 = 9
CHUNKS = [(0, 512), (512, 512), (1024, 512), (1536, C_ALL - 1536)]

NQ, KS, KW, DQ, KDD, IQ, IK, KC, VC = 0, 4, 5, 6, 8, 9, 11, 12, 14
SLOTS = 16

COUNT = [TK // (i + 1) for i in range(TK)]
OFF = [sum(COUNT[:i]) for i in range(TK)]
NCAND = sum(COUNT)
RUNS = []
for _i in range(TK):
    if RUNS and RUNS[-1][2] == COUNT[_i]:
        RUNS[-1] = (RUNS[-1][0], RUNS[-1][1] + 1, COUNT[_i])
    else:
        RUNS.append((_i, 1, COUNT[_i]))

K_ID, K_IOTA, K_TRI, K_CB, K_FREQ = 0, 128, 256, 512, 512 + T * NC
K_ALL = K_FREQ + 12


def constants():
    c = np.zeros((P, K_ALL), np.float32)
    c[:, K_ID:K_ID + P] = np.eye(P, dtype=np.float32)
    c[:, K_IOTA:K_IOTA + P] = np.arange(P, dtype=np.float32)
    row = np.arange(P)[:, None]
    c[:, K_TRI + P:K_TRI + 2 * P] = np.where(np.arange(P)[None, :] <= row, 0.0, NEG)
    for t in range(T):
        end = np.arange(NC)[None, :] * CMP_STRIDE + CMP_LEN - 1
        c[:, K_CB + t * NC:K_CB + (t + 1) * NC] = np.where(end <= row + t * P, 0.0, NEG)
    for at, half in ((0, 8), (8, 4)):
        c[:, K_FREQ + at:K_FREQ + at + half] = (500000.0 ** (-np.arange(half) / half)).astype(np.float32)
    return c


A_WIN = 0
A_WQA = 0
A_TT = 8192
A_X = A_TT + SLOTS * S
A_PT = A_X + 2 * 1024
A_END1 = A_PT + 2 * 1024
A_OT = A_TT
A_WQB = 8192
A_XT = 16384
A_S = A_XT + 2048
A_WOUT = KD * (C_ALL + 256)
A_H = A_WOUT + KD * D
A_MQ = A_H + T * C_ALL
A_RT = A_MQ + 1536
A_QT = A_S + 4096
A_V = A_QT + 512
A_I = A_V + 512
A_R = A_I + 512
A_ALL = 32768


def peer_layer_kernel(nc, x, xT, memT, positions, w_tok, w_memq, w_memk, w_memv, w1k, w1v, w2k, w2v, peT,
                      w_out, ln1, wqa, wqb, subk, uT, pv, ln2, consts, out):
    with ExitStack() as ctx:
        def sb(name, shape, dt=F32):
            return ctx.enter_context(nc.sbuf_tensor(name, shape, dt))

        def sem(name):
            return ctx.enter_context(nc.semaphore(name))

        arena = sb("arena", [P, A_ALL])
        slab_at = nc.sbuf_base
        slab = sb("slab", [P, 4 * 4096 + 128])
        raw = slab[:, 0:8192].rearrange("p (b a n) -> p b a n", b=RB, a=2)
        lo = nc.alloc_sbuf_tensor_at("lo", [P, RB, 2, 1024], F32R, offset=slab_at)
        hi = nc.alloc_sbuf_tensor_at("hi", [P, 2, 2, 1024], F32R, offset=slab_at + 4 * 8320)
        x1hl = nc.alloc_sbuf_tensor_at("x1hl", [P, KD, 2, S], F32R, offset=slab_at + 4 * 12416)
        xs = sb("xs", [P, T, D])
        ahl = sb("ahl", [P, 2, 2, S], F32R)
        gel = sb("gel", [P, 2, S])
        oh = slab[:, 4096:6144].rearrange("p (b a q n) -> p b a q n", b=2, a=2, q=4)
        kc = slab[:, 6144:6144 + K_ALL]
        sm = slab[:, 6144 + K_ALL:8320]
        n2 = sb("n2", [P, 2, 4])
        lnst = sb("lnst", [P, T, 8])
        pos_i = sb("pos_i", [P, T], I32)
        ps = ctx.enter_context(nc.psum_tensor("ps", [P, 8, 512], F32))

        def ar(at, n):
            return arena[:, at:at + n]

        ident = kc[:, K_ID:K_ID + P]
        iota = kc[:, K_IOTA:K_IOTA + P]

        at = [0]

        def small(n):
            at[0] += n
            assert at[0] <= 8320 - 6144 - K_ALL
            return sm[:, at[0] - n:at[0]]

        posf = small(T)
        ang = small(T * 12).rearrange("p (t f) -> p t f", t=T)
        turns = small(T * 12).rearrange("p (t f) -> p t f", t=T)
        cosv = small(T * 12).rearrange("p (t f) -> p t f", t=T)
        sinv = small(T * 12).rearrange("p (t f) -> p t f", t=T)
        gate = small(T * 24).rearrange("p (t h b) -> p t h b", t=T, b=3)
        iw = small(T * 8).rearrange("p (t h) -> p t h", t=T)
        kcT = small(16)
        cmax = small(8)
        gmax = small(16)
        gneg = small(16)
        gden = small(16)
        grec = small(16)
        gcoef = small(16)
        slotT = small(3 * S).rearrange("p (a t) -> p a t", a=3)
        pe_sb = small(2 * LP).rearrange("p (a l) -> p a l", a=2)
        w2k_sb = oh[:, 1, 1, 0, :]
        w2v_sb = oh[:, 1, 1, 1, 0:HD]
        subk_sb = small(2 * P).rearrange("p (a n) -> p a n", a=2)

        dup = oh[:, :, :, :, :].rearrange("p a b c d -> p (a b c d)")[:, 0:1536].rearrange(
            "p (t n) -> p t n", t=T)
        w_t = ar(A_WIN, KD * C_ALL).rearrange("p (k n) -> p k n", k=KD)
        w_mq = ar(A_WIN + KD * C_ALL, KD * 256).rearrange("p (k n) -> p k n", k=KD)
        w_o = ar(A_WOUT, KD * D).rearrange("p (k n) -> p k n", k=KD)
        h = ar(A_H, T * C_ALL).rearrange("p (t n) -> p t n", t=T)
        mq = ar(A_MQ, 1536).rearrange("p (a b s) -> p a b s", a=3, b=2)
        rawf = slab[:, 0:4096]
        w_mk = rawf[:, 0:2048].rearrange("p (k n) -> p k n", k=KD)
        w_mv = rawf[:, 2048:4096].rearrange("p (k n) -> p k n", k=KD)
        xhf = slab[:, 12416:16512]
        memT_sb = xhf[:, 0:2048].rearrange("p (k n) -> p k n", k=KD)
        xT_sb = xhf[:, 2048:4096].rearrange("p (k n) -> p k n", k=KD)
        hif = slab[:, 8320:12416]
        w1 = hif[:, 0:4096].rearrange("p (a l n) -> p a l n", a=2, l=LP)
        ln_sb = hif[:, 0:2048].rearrange("p (a n) -> p a n", a=2)
        rt = ar(A_RT, 1120)
        TT = ar(A_TT, SLOTS * S).rearrange("p (s t) -> p s t", s=SLOTS)
        xb = ar(A_X, 2048).rearrange("p (b j n) -> p b j n", b=2, j=4)
        PT = ar(A_PT, 2048).rearrange("p (b j n) -> p b j n", b=2, j=4)
        oT = ar(A_OT, 2048).rearrange("p (k t) -> p k t", k=KD)
        ocs = [oh[:, 1 - t, :, :, :].rearrange("p a b c -> p (a b c)") for t in range(T)]
        flat = ar(A_RT, 960).rearrange("p (a l g b) -> p a l g b", a=2, l=LP, g=2)
        CX = A_END1
        assert CX + 1536 <= A_WOUT
        ghk = ar(CX, 32)
        ghv = ar(CX + 32, 256).rearrange("p (g j b) -> p g j b", g=2, j=4)
        vbd = ar(CX + 288, 512).rearrange("p (g j n) -> p g j n", g=2, j=4)
        pc = ar(CX + 800, 120).rearrange("p (h b) -> p h b", h=8)
        pcp = ar(CX + 920, 256).rearrange("p (h b) -> p h b", h=8)
        score = oh[:, 0, 0, :, :].rearrange("p a b -> p (a b)").rearrange("p (t s) -> p t s", t=T)
        dbias = oh[:, 0, 1, :, :].rearrange("p a b -> p (a b)").rearrange("p (t s) -> p t s", t=T)
        rl = PT
        pcT = ar(CX + 1176, 256).rearrange("p (g t) -> p g t", g=2)
        top8 = gcoef[:, 0:8]

        x1T = ar(A_XT, 2048).rearrange("p (k t) -> p k t", k=KD)
        wq_sb = [ar(A_WQA, 8192).rearrange("p (k n) -> p k n", k=KD),
                 ar(A_WQB, 8192).rearrange("p (k n) -> p k n", k=KD)]
        sc = ar(A_S, 4096).rearrange("p (t b n) -> p t b n", t=T, b=2 * PH)
        qT = ar(A_QT, 512).rearrange("p (b t) -> p b t", b=2)
        V = ar(A_V, 512).rearrange("p (t b k) -> p t b k", t=T, b=2 * PH)
        IX = ar(A_I, 512).bitcast(U32).rearrange("p (t b k) -> p t b k", t=T, b=2 * PH)
        IF = ar(A_R, 256).rearrange("p (b k) -> p b k", b=2 * PH)
        cand = ar(A_R + 256, PH * NCAND).rearrange("p (h c) -> p h c", h=PH)
        cande = ar(A_R + 656, PH * NCAND).rearrange("p (h c) -> p h c", h=PH)
        tv = ar(A_R + 1056, 128).rearrange("p (h k) -> p h k", h=PH)
        ti = ar(A_R + 1184, 128).bitcast(U32).rearrange("p (h k) -> p h k", h=PH)
        junk = ar(A_H, 2048).rearrange("p (t n) -> p t n", t=T)
        tf = ar(A_R + 1312, 128).rearrange("p (h k) -> p h k", h=PH)
        ex = ar(A_R + 1440, 384).rearrange("p (a s) -> p a s", a=3)
        te = ar(A_R + 1824, 128).rearrange("p (h k) -> p h k", h=PH)
        gs = ar(A_R + 1952, 16)
        eq = ar(A_R + 1968, PH * TK * NCAND)
        assert A_R + 1968 + PH * TK * NCAND <= A_ALL
        G = arena[:, :].rearrange("p (c t) -> p c t", c=NK)
        ln2_sb = ar(0, 2048).rearrange("p (a n) -> p a n", a=2)

        l_const, l_pos, l_pe, l_x = sem("l_const"), sem("l_pos"), sem("l_pe"), sem("l_x")
        l_xT, l_mT, l_wmk, l_wmv, l_wmq = (sem(n) for n in ("l_xT", "l_mT", "l_wmk", "l_wmv", "l_wmq"))
        l_w = [sem(f"l_wtok{n}") for n in range(len(CHUNKS))]
        l_w1, l_w2, l_wo, l_ln1 = sem("l_w1"), sem("l_w2"), sem("l_wo"), sem("l_ln1")
        l_wqa, l_wqb, l_sk, l_ln2 = sem("l_wqa"), sem("l_wqb"), sem("l_sk"), sem("l_ln2")
        pe_proj, h_saved = sem("pe_proj"), sem("h_saved")
        pe_memp, mem_saved = sem("pe_memp"), sem("mem_saved")
        dve_chain = sem("dve_chain")
        ang_ready, trig = sem("ang_ready"), sem("trig")
        roped = sem("roped")
        gate_exp = sem("gate_exp")
        pe_tr, tr_saved = sem("pe_tr"), sem("tr_saved")
        flat_ready, pe_hid, hid_act = sem("flat_ready"), sem("pe_hid"), sem("hid_act")
        pad_zero, pe_kv, kv_saved = sem("pad_zero"), sem("pe_kv"), sem("kv_saved")
        pe_idx, relu_done, idx_read = sem("pe_idx"), sem("relu_done"), sem("idx_read")
        pe_cs, cx_ready, cx_exp, cp_ready = sem("pe_cs"), sem("cx_ready"), sem("cx_exp"), sem("cp_ready")
        pe_cT, cT_saved = sem("pe_cT"), sem("cT_saved")
        pe_s, neg_ready, exp_done, prob_ready = sem("pe_s"), sem("neg_ready"), sem("exp_done"), sem("prob_ready")
        pe_pT, pT_saved, pe_pv = sem("pe_pT"), sem("pT_saved"), sem("pe_pv")
        o_saved, pe_oT, oT_saved, pe_mix = sem("o_saved"), sem("pe_oT"), sem("oT_saved"), sem("pe_mix")
        centred, squared, var_ready, rooted = sem("centred"), sem("squared"), sem("var_ready"), sem("rooted")
        x1_ready, pe_xT, xT_saved, x1_split = sem("x1_ready"), sem("pe_xT"), sem("xT_saved"), sem("x1_split")
        pe_q, q_saved, pe_sk, sk_saved = sem("pe_q"), sem("q_saved"), sem("pe_sk"), sem("sk_saved")
        g_shift, g_exp, route_ready = sem("g_shift"), sem("g_exp"), sem("route_ready")
        pe_rT, rT_saved = sem("pe_rT"), sem("rT_saved")
        n2_ready, n2_seen, oh2_ready = sem("n2_ready"), sem("n2_seen"), sem("oh2_ready")
        oh_ready, pe_g, g_saved = sem("oh_ready"), sem("pe_g"), sem("g_saved")
        u_in = [sem(f"u_in{b}") for b in range(RB)]
        v_in = [sem(f"v_in{b}") for b in range(RB)]
        u_hi, u_lo, v_hi, v_lo = sem("u_hi"), sem("u_lo"), sem("v_hi"), sem("v_lo")
        pe_h, gelu_done, gated, a_hi, a_lo, pe_y = (sem(n) for n in ("pe_h", "gelu_done", "gated", "a_hi", "a_lo", "pe_y"))
        y_ready, stored = sem("y_ready"), sem("stored")

        KINDS = [("sel", 0), ("sel", 1), ("win", 0), ("win", 1), ("mem", 0), ("dsa", 0)]
        GROUPS = [(t, k, g) for t in range(T) for k, g in KINDS]

        def width(t, k):
            return MEM if k == "mem" else P * (t + 1)

        def place(j):
            return (j % 2) * 2 + j // 2

        def bank2(b):
            return ps[:, 2 * b:2 * b + 2, :].rearrange("p a n -> p (a n)")

        block = ctx.enter_context(nc.Block())

        @block.sync
        def _(sp):
            sp.dma_start(xT_sb, xT).then_inc(l_xT, 16)
            for n, (c0, w) in enumerate(CHUNKS):
                sp.dma_start(w_t[:, :, c0:c0 + w], w_tok[:, :, c0:c0 + w]).then_inc(l_w[n], 16)
            sp.dma_start(w_mq, w_memq).then_inc(l_wmq, 16)
            sp.dma_start(memT_sb, memT).then_inc(l_mT, 16)
            sp.dma_start(w_mk, w_memk).then_inc(l_wmk, 16)
            sp.dma_start(w_mv, w_memv).then_inc(l_wmv, 16)
            sp.dma_start(w1[:, 0], w1k).then_inc(l_w1, 16)
            sp.dma_start(w1[:, 1], w1v).then_inc(l_w1, 16)
            sp.dma_start(w_o, w_out).then_inc(l_wo, 16)
            sp.wait_ge(pe_proj, T * len(CHUNKS))
            sp.dma_start(wq_sb[0], wqa).then_inc(l_wqa, 16)
            sp.wait_ge(pe_hid, 2)
            sp.dma_start(ln_sb, ln1.partition_broadcast(P)).then_inc(l_ln1, 16)
            sp.wait_ge(pe_mix, 2)
            sp.dma_start(wq_sb[1], wqb).then_inc(l_wqb, 16)
            sp.wait_ge(pe_memp, 6)

            def load(i, b, first):
                if not first:
                    sp.wait_ge(pe_h, i * RB + (b - RB + 1))
                c = bass.ds(i * RB + b, 1)
                sp.dma_start(raw[:, b, 0, :], uT[c].rearrange("o p n -> (o p) n")).then_inc(u_in[b], 16)
                if not first:
                    sp.wait_ge(pe_y, i * RB + (b - RB + 1))
                sp.dma_start(raw[:, b, 1, :], pv[c].rearrange("o p n -> (o p) n")).then_inc(v_in[b], 16)

            for b in range(RB):
                if b == 2:
                    sp.wait_ge(pe_g, 2 * (S // 8))
                load(0, b, True)
            with sp.Fori(1, NK // RB) as i:
                for b in range(RB):
                    load(i, b, False)
            for t in range(T):
                sp.wait_ge(y_ready, t + 1)
                sp.dma_start(out[t * P:(t + 1) * P, :], xs[:, t, :]).then_inc(stored, 16)
            sp.wait_ge(stored, 16 * T)

        @block.gpsimd
        def _(pool):
            pool.dma_start(kc[:, :], consts).then_inc(l_const, 16)
            pool.dma_start(pos_i[:, :], positions).then_inc(l_pos, 16)
            pool.dma_start(pe_sb, peT).then_inc(l_pe, 16)
            pool.dma_start(w2k_sb, w2k).then_inc(l_w2, 16)
            pool.dma_start(w2v_sb, w2v).then_inc(l_w2, 16)
            pool.dma_start(subk_sb, subk).then_inc(l_sk, 16)
            pool.dma_start(xs[:, :, :], x).then_inc(l_x, 16)

            def chunk(i):
                for b in range(2):
                    c = i * 2 + b
                    pool.wait_ge(gelu_done, c + 1)
                    nc.gpsimd.tensor_tensor(out=gel[:, b, :], in0=gel[:, b, :],
                                            in1=G[:, bass.ds(c, 1), :].rearrange("p o t -> p (o t)"),
                                            op=ALU.mult).then_inc(gated, 1)

            def onehots(i, first):
                for b in range(2):
                    nc.gpsimd.tensor_copy(n2[:, b, :], slotT[:, 1, bass.ds(i * 8 + b * 4, 4)]).then_inc(n2_ready, 1)
                    if not first:
                        pool.wait_ge(pe_g, i * 2 + (b - 1))
                    pool.wait_ge(n2_ready, i * 2 + (b + 1))
                    pool.sem_inc(n2_seen, 1)
                    for q in range(POOL_HOT):
                        ins = nc.gpsimd.tensor_scalar(oh[:, b, 0, q, :], iota, n2[:, b, q:q + 1], None, ALU.is_equal)
                    ins.then_inc(oh2_ready, 1)

            pool.wait_ge(rT_saved, T)
            onehots(0, True)
            with pool.Fori(1, S // 8) as i:
                onehots(i, False)
            pool.wait_ge(g_saved, 2 * (S // 8))
            with pool.Fori(0, NK // 2) as i:
                chunk(i)
            pool.wait_ge(gated, NK)
            pool.dma_start(ln2_sb, ln2.partition_broadcast(P)).then_inc(l_ln2, 16)

        @block.tensor
        def _(pe):
            def mm(o, lhsT, rhs, start, stop):
                return nc.tensor.matmul(o, lhsT, rhs, start=start, stop=stop, skip_group_check=True)

            pe.wait_ge(l_xT, 16)
            for t in range(T):
                for n, (c0, w) in enumerate(CHUNKS):
                    pe.wait_ge(l_w[n], 16)
                    for k in range(KD):
                        last = mm(ps[:, t * 4 + n, 0:w], xT_sb[:, k, t * P:(t + 1) * P], w_t[:, k, c0:c0 + w],
                                  k == 0, k == KD - 1)
                    last.then_inc(pe_proj, 1)

            pe.wait_ge(l_wmq, 16)
            pe.wait_ge(l_mT, 16)
            pe.wait_ge(l_wmk, 16)
            pe.wait_ge(l_wmv, 16)
            pe.wait_ge(h_saved, 6)
            for m in range(6):
                a, b = m // 2, m % 2
                for k in range(KD):
                    if a == 0:
                        ops = (w_mq[:, k, b * P:(b + 1) * P], xT_sb[:, k, :])
                    elif a == 1:
                        ops = (w_mk[:, k, b * P:(b + 1) * P], memT_sb[:, k, :])
                    else:
                        ops = (memT_sb[:, k, b * P:(b + 1) * P], w_mv[:, k, :])
                    last = mm(ps[:, m, 0:S], *ops, k == 0, k == KD - 1)
                last.then_inc(pe_memp, 1)

            src = ([("h", C_NQ + P * j) for j in range(4)] + [("h", C_KS), ("h", C_KW), ("h", C_DQ), ("h", C_DQ + P)]
                   + [("d", 0), ("h", C_IQ), ("h", C_IQ + P), ("d", 128)] + [("d", 256 + P * j) for j in range(4)])
            pe.wait_ge(h_saved, 8)
            pe.wait_ge(mem_saved, 6)
            pe.wait_ge(l_const, 16)
            for t in range(T):
                pe.wait_ge(roped, t + 1)
                for s, (kind, c0) in enumerate(src):
                    a = h[:, t, c0:c0 + P] if kind == "h" else dup[:, t, c0:c0 + P]
                    last = nc.tensor.transpose(ps[:, t * 4 + s // 4, (s % 4) * P:(s % 4 + 1) * P], a, ident)
                    if s % 4 == 3:
                        last.then_inc(pe_tr, 1)

            pe.wait_ge(l_w1, 32)
            pe.wait_ge(tr_saved, 8)
            for a in range(2):
                pe.wait_ge(flat_ready, a + 1)
                for l in range(LP):
                    last = mm(ps[:, a, 0:2 * NC], w1[:, a, l, :],
                              flat[:, a, l, :, :].rearrange("p g b -> p (g b)"), l == 0, l == LP - 1)
                last.then_inc(pe_hid, 1)
            pe.wait_ge(l_w2, 32)
            pe.wait_ge(hid_act, 3)
            mm(ps[:, 2, 0:2 * NC], w2k_sb, ghk[:, 0:2 * NC], True, True).then_inc(pe_kv, 1)
            for g in range(2):
                mm(ps[:, 3 + g, 0:HD], ghv[:, g, :, :].rearrange("p j b -> p (j b)"), w2v_sb,
                   True, True).then_inc(pe_kv, 1)

            pe.wait_ge(kv_saved, 3)
            for t in range(T):
                if t:
                    pe.wait_ge(relu_done, 8)
                w = width(t, "idx")
                for i in range(IDX_H):
                    r = slice(32 * (i % 4), 32 * (i % 4) + 32)
                    last = mm(ps[:, i % 4, (i // 4) * S:(i // 4) * S + w],
                              TT[r, IQ + i // 4, t * P:(t + 1) * P], TT[r, IK, 0:w], i < 4, True)
                last.then_inc(pe_idx, 1)

            def cmp_scores(t):
                for hh in range(8):
                    g, j = hh // 4, hh % 4
                    last = mm(ps[:, 4 + g, j * 16:j * 16 + NC], TT[64 * g:64 * g + 64, NQ + j, t * P:(t + 1) * P],
                              kcT[64 * g:64 * g + 64, 0:NC], j == 0, True)
                last.then_inc(pe_cs, 1)

            def cmp_out(t):
                pe.wait_ge(cp_ready, t + 1)
                for g in range(2):
                    last = nc.tensor.transpose(ps[:, 4 + g, 0:P],
                                               pcp[:, 4 * g:4 * g + 4, :].rearrange("p h b -> p (h b)"), ident)
                last.then_inc(pe_cT, 1)
                pe.wait_ge(cT_saved, t + 1)
                for g in range(2):
                    mm(ps[:, 6, g * S:(g + 1) * S], pcT[:, g, :],
                       vbd[:, g, :, :].rearrange("p j n -> p (j n)"), g == 0, False)

            def scores(n):
                t, k, g = GROUPS[n]
                w = width(t, k)
                if n >= 2:
                    if GROUPS[n - 2][1] == "mem":
                        pe.wait_ge(exp_done, 4 * (n - 1))
                    else:
                        pe.wait_ge(neg_ready, n - 1)
                for j in range(4):
                    q0, q1 = t * P, (t + 1) * P
                    if k in ("sel", "win"):
                        r = slice(64 * g, 64 * g + 64)
                        ops = (TT[r, NQ + j, q0:q1], TT[r, KS if k == "sel" else KW, 0:w])
                    elif k == "dsa":
                        r = slice(64 * (j % 2), 64 * (j % 2) + 64)
                        ops = (TT[r, DQ + j // 2, q0:q1], TT[r, KDD, 0:w])
                    else:
                        r = slice(64 * (j % 2), 64 * (j % 2) + 64)
                        ops = (mq[r, 0, j // 2, q0:q1], mq[r, 1, j // 2, :])
                    pl = place(j)
                    last = mm(ps[:, 2 * (n % 2) + pl // 2, (pl % 2) * S:(pl % 2) * S + w], *ops, pl % 2 == 0, True)
                last.then_inc(pe_s, 1)

            def turn(n):
                t, k, g = GROUPS[n]
                nb = width(t, k) // P
                pe.wait_ge(prob_ready, n + 1)
                if n >= 1:
                    pe.wait_ge(pT_saved, n)
                for j in range(4):
                    for b in range(nb):
                        q = j * nb + b
                        last = nc.tensor.transpose(ps[:, 4 + q // 4, (q % 4) * P:(q % 4 + 1) * P],
                                                   xb[:, n % 2, j, b * P:(b + 1) * P], ident)
                last.then_inc(pe_pT, 1)

            def outputs(n):
                t, k, g = GROUPS[n]
                nb = width(t, k) // P
                pe.wait_ge(pT_saved, n + 1)
                for j in range(4):
                    for b in range(nb):
                        if k == "sel":
                            v = h[:, b, C_VS + g * HD:C_VS + (g + 1) * HD]
                        elif k == "win":
                            v = h[:, b, C_VW + g * HD:C_VW + (g + 1) * HD]
                        elif k == "dsa":
                            v = h[:, b, C_VD:C_VD + HD]
                        else:
                            v = mq[:, 2, b, j * HD:(j + 1) * HD]
                        if k in ("sel", "win"):
                            o = ps[:, 6, (4 * g + j) * HD:(4 * g + j + 1) * HD]
                        else:
                            c0 = (0 if k == "dsa" else S) + j * HD
                            o = ps[:, 7, c0:c0 + HD]
                        last = mm(o, PT[:, n % 2, j, b * P:(b + 1) * P], v,
                                  k == "mem" and j == 0 and b == 0, True)
                last.then_inc(pe_pv, 1)

            for t in range(T):
                if t == 0:
                    cmp_scores(0)
                    pe.wait_ge(relu_done, 16)
                    scores(0)
                else:
                    pe.wait_ge(pT_saved, len(KINDS) * t)
                    cmp_scores(t)
                if t:
                    pe.wait_ge(o_saved, 2 * t)
                cmp_out(t)
                for n in range(t * len(KINDS), (t + 1) * len(KINDS)):
                    if n + 1 < len(GROUPS):
                        scores(n + 1)
                    turn(n)
                    if n % len(KINDS):
                        outputs(n - 1)
                outputs((t + 1) * len(KINDS) - 1)

            for t in range(T):
                pe.wait_ge(o_saved, 2 * t + 2)
                if t == 0:
                    pe.wait_ge(exp_done, 4 * len(GROUPS))
                for k in range(KD):
                    last = nc.tensor.transpose(ps[:, 2 * t + k // 4, (k % 4) * P:(k % 4 + 1) * P],
                                               ocs[t][:, k * P:(k + 1) * P], ident)
                last.then_inc(pe_oT, 1)
            pe.wait_ge(l_wo, 16)
            for t in range(T):
                pe.wait_ge(oT_saved, t + 1)
                for half in range(2):
                    for k in range(KD):
                        last = mm(ps[:, 4 + 2 * t + half, :], oT[:, k, t * P:(t + 1) * P],
                                  w_o[:, k, half * 512:(half + 1) * 512], k == 0, k == KD - 1)
                last.then_inc(pe_mix, 1)

            for t in range(T):
                pe.wait_ge(x1_ready, t + 1)
                for k in range(KD):
                    last = nc.tensor.transpose(ps[:, 2 * t + k // 4, (k % 4) * P:(k % 4 + 1) * P],
                                               xs[:, t, k * P:(k + 1) * P], ident)
                last.then_inc(pe_xT, 1)

            pe.wait_ge(l_wqa, 16)
            pe.wait_ge(l_sk, 16)
            pe.wait_ge(xT_saved, 2)

            def subkey_scores(b):
                pe.wait_ge(q_saved, b + 1)
                if b >= 2:
                    pe.wait_ge(sk_saved, b - 1)
                for t in range(T):
                    last = mm(ps[:, 6 + b % 2, t * P:(t + 1) * P], qT[:, b % 2, t * P:(t + 1) * P],
                              subk_sb[:, b % 2, :], t == 0, True)
                last.then_inc(pe_sk, 1)

            for b in range(2 * PH):
                if b == PH:
                    pe.wait_ge(l_wqb, 16)
                if b >= 2:
                    pe.wait_ge(q_saved, b - 1)
                for k in range(KD):
                    last = mm(ps[:, 4 + b % 2, 0:S], wq_sb[b // PH][:, k, (b % PH) * P:(b % PH + 1) * P],
                              x1T[:, k, :], k == 0, k == KD - 1)
                last.then_inc(pe_q, 1)
                if b >= 1:
                    subkey_scores(b - 1)
            subkey_scores(2 * PH - 1)

            for t in range(T):
                pe.wait_ge(route_ready, t + 1)
                for a in range(3):
                    last = nc.tensor.transpose(ps[:, t, a * P:(a + 1) * P], ex[:, a, :], ident)
                last.then_inc(pe_rT, 1)

            def gates(i, first):
                for b in range(2):
                    pe.wait_ge(oh_ready, i * 2 + (b + 1))
                    pe.wait_ge(oh2_ready, i * 2 + (b + 1))
                    if not first:
                        pe.wait_ge(g_saved, i * 2 + (b - 1))
                    for q in range(4):
                        last = mm(ps[:, 2 + b, q * P:(q + 1) * P], oh[:, b, 0, q, :], oh[:, b, 1, q, :],
                                  q == 0, True)
                    last.then_inc(pe_g, 1)

            gates(0, True)
            with pe.Fori(1, S // 8) as i:
                gates(i, False)

            def expert_in(i, b, first):
                pe.wait_ge(u_lo, i * RB + (b + 1))
                if not first:
                    pe.wait_ge(gelu_done, i * RB + (b - 1))
                for k in range(KD):
                    ks = slice(k * P, (k + 1) * P)
                    ws = ((hi[:, b % 2, 0, ks], 0), (hi[:, b % 2, 0, ks], 1), (lo[:, b % RB, 0, ks], 0))
                    for m, (w, part) in enumerate(ws):
                        last = mm(ps[:, b % 2, 0:S], w, x1hl[:, k, part, :], k == 0 and m == 0,
                                  k == KD - 1 and m == 2)
                last.then_inc(pe_h, 1)

            def expert_out(i, b, first, final):
                pe.wait_ge(v_lo, i * RB + (b + 1))
                pe.wait_ge(a_lo, i * RB + (b + 1))
                for t in range(T):
                    vs = ((0, hi[:, b % 2, 1, :]), (0, lo[:, b % RB, 1, :]), (1, hi[:, b % 2, 1, :]))
                    for m, (part, v) in enumerate(vs):
                        for half in range(2):
                            last = mm(ps[:, 4 + 2 * t + half, :], ahl[:, b % 2, part, t * P:(t + 1) * P],
                                      v[:, half * 512:(half + 1) * 512], first and m == 0, final and m == 2)
                last.then_inc(pe_y, 1)

            pe.wait_ge(rT_saved, 2)
            pe.wait_ge(x1_split, 2)
            for b in range(RB):
                expert_in(0, b, b < 2)
                if b:
                    expert_out(0, b - 1, b == 1, False)
            with pe.Fori(1, NK // RB) as i:
                for b in range(RB):
                    expert_in(i, b, False)
                    expert_out(i, b - 1, False, False)
            expert_out(NK // RB - 1, RB - 1, False, True)

        @block.scalar
        def _(act):
            act.wait_ge(ang_ready, 1)
            nc.scalar.activation(sinv, turns, ACT.Sin).then_inc(trig, 1)
            nc.scalar.activation(cosv, ang, ACT.Sin).then_inc(trig, 1)
            for t in range(T):
                for n, (c0, w) in enumerate(CHUNKS):
                    act.wait_ge(pe_proj, t * 4 + n + 1)
                    nc.scalar.copy(h[:, t, c0:c0 + w], ps[:, t * 4 + n, 0:w]).then_inc(h_saved, 1)
                nc.scalar.activation(gate[:, t, :, :].rearrange("p h b -> p (h b)"),
                                     ps[:, t * 4 + 3, C_GATE - 1536:C_GATE - 1536 + 24], ACT.Exp, scale=-1.0
                                     ).then_inc(gate_exp, 1)
            for m in range(6):
                act.wait_ge(pe_memp, m + 1)
                nc.scalar.copy(mq[:, m // 2, m % 2, :], ps[:, m, 0:S]).then_inc(mem_saved, 1)

            for t in range(T):
                for q in range(4):
                    act.wait_ge(pe_tr, t * 4 + q + 1)
                    v = ps[:, t * 4 + q, :].rearrange("p (s n) -> p s n", s=4)
                    if q < 3:
                        nc.scalar.copy(TT[:, 4 * q:4 * q + 4, t * P:(t + 1) * P], v).then_inc(tr_saved, 1)
                    else:
                        nc.scalar.copy(TT[0:64, 12:16, t * P:(t + 1) * P], v[0:64])
                        if t == 0:
                            nc.scalar.copy(TT[64:128, 12:16, 0:P - 1], v[64:128, :, 1:P]).then_inc(tr_saved, 1)
                        else:
                            nc.scalar.copy(TT[64:128, 12:16, P - 1:2 * P - 1], v[64:128]).then_inc(tr_saved, 1)

            act.wait_ge(pad_zero, 1)
            act.wait_ge(pe_hid, 1)
            nc.scalar.activation(ghk[:, 0:2 * NC], ps[:, 0, 0:2 * NC], ACT.Gelu).then_inc(hid_act, 1)
            act.wait_ge(pe_hid, 2)
            for g in range(2):
                nc.scalar.activation(ghv[:, g, :, 0:NC],
                                     ps[:, 1, g * NC:(g + 1) * NC].unsqueeze(1).to_broadcast([P, 4, NC]),
                                     ACT.Gelu).then_inc(hid_act, 1)

            for t in range(T):
                w = width(t, "idx")
                act.wait_ge(pe_idx, t + 1)
                if t:
                    act.wait_ge(idx_read, 8)
                for i in range(IDX_H):
                    nc.scalar.activation(rl[:, i // 4, i % 4, 0:w],
                                         ps[:, i % 4, (i // 4) * S:(i // 4) * S + w], ACT.Relu).then_inc(relu_done, 1)

            def cmp_exp(t):
                act.wait_ge(cx_ready, t + 1)
                nc.scalar.activation(pc, pc, ACT.Exp, scale=SCALE).then_inc(cx_exp, 1)

            def save_o(t):
                act.wait_ge(pe_pv, (t + 1) * len(KINDS))
                for half in range(2):
                    nc.scalar.copy(ocs[t][:, half * 512:(half + 1) * 512], ps[:, 6 + half, :]).then_inc(o_saved, 1)

            act.wait_ge(idx_read, 16)
            for n, (t, k, g) in enumerate(GROUPS):
                w = width(t, k)
                if n % len(KINDS) == 0:
                    cmp_exp(t)
                act.wait_ge(neg_ready, n + 1)
                for j in range(4):
                    c = 4 * (n % 2) + j
                    pl = place(j)
                    src = (ps[:, 2 * (n % 2) + pl // 2, (pl % 2) * S:(pl % 2) * S + w] if k == "mem"
                           else xb[:, n % 2, j, 0:w])
                    nc.scalar.activation(xb[:, n % 2, j, 0:w], src, ACT.Exp, bias=gneg[:, c:c + 1], scale=SCALE,
                                         accum_out=gden[:, c:c + 1]).then_inc(exp_done, 1)
                if n % len(KINDS) == 0:
                    act.wait_ge(pe_cT, t + 1)
                    nc.scalar.copy(pcT, ps[:, 4:6, 0:P]).then_inc(cT_saved, 1)
                act.wait_ge(pe_pT, n + 1)
                if n >= 2:
                    act.wait_ge(pe_pv, n - 1)
                nc.scalar.copy(PT[:, n % 2, :, 0:w],
                               bank2(2)[:, 0:4 * w].rearrange("p (j n) -> p j n", j=4)).then_inc(pT_saved, 1)
                if n % len(KINDS) == len(KINDS) - 1:
                    save_o(t)

            for t in range(T):
                act.wait_ge(pe_oT, t + 1)
                nc.scalar.copy(oT[:, :, t * P:(t + 1) * P],
                               bank2(t).rearrange("p (k n) -> p k n", k=KD)).then_inc(oT_saved, 1)

            def norm(n, t):
                act.wait_ge(centred, n * T + t + 1)
                nc.scalar.activation(junk[:, t, :], xs[:, t, :], ACT.Square,
                                     accum_out=lnst[:, t, 2:3]).then_inc(squared, 1)
                act.wait_ge(var_ready, n * T + t + 1)
                nc.scalar.activation(lnst[:, t, 4:5], lnst[:, t, 3:4], ACT.Sqrt).then_inc(rooted, 1)

            for t in range(T):
                norm(0, t)
            for t in range(T):
                act.wait_ge(pe_xT, t + 1)
                nc.scalar.copy(x1T[:, :, t * P:(t + 1) * P],
                               bank2(t).rearrange("p (k n) -> p k n", k=KD)).then_inc(xT_saved, 1)

            def save_scores(b):
                act.wait_ge(pe_sk, b + 1)
                nc.scalar.copy(sc[:, :, b, :], ps[:, 6 + b % 2, 0:S].rearrange("p (t n) -> p t n", t=T)
                               ).then_inc(sk_saved, 1)

            for b in range(2 * PH):
                act.wait_ge(pe_q, b + 1)
                if b >= 2:
                    act.wait_ge(pe_sk, b - 1)
                nc.scalar.copy(qT[:, b % 2, :], ps[:, 4 + b % 2, 0:S]).then_inc(q_saved, 1)
                if b >= 1:
                    save_scores(b - 1)
            save_scores(2 * PH - 1)

            for t in range(T):
                act.wait_ge(g_shift, t + 1)
                nc.scalar.activation(te, te, ACT.Exp).then_inc(g_exp, 1)
                act.wait_ge(pe_rT, t + 1)
                nc.scalar.copy(slotT[:, :, t * P:(t + 1) * P],
                               ps[:, t, 0:3 * P].rearrange("p (a n) -> p a n", a=3)).then_inc(rT_saved, 1)

            def save_gates(i):
                for b in range(2):
                    act.wait_ge(pe_g, i * 2 + (b + 1))
                    nc.scalar.copy(G[:, :, bass.ds(i * 8 + b * 4, 4)].rearrange("p c q -> p q c"),
                                   ps[:, 2 + b, :].rearrange("p (q c) -> p q c", q=4)).then_inc(g_saved, 1)

            with act.Fori(0, S // 8) as i:
                save_gates(i)

            def u_split(i, b, first):
                act.wait_ge(u_in[b], (i + 1) * 16)
                if not first:
                    act.wait_ge(pe_h, i * RB + (b - 1))
                nc.scalar.copy(hi[:, b % 2, 0, :], raw[:, b, 0, :]).then_inc(u_hi, 1)

            def v_split(i, b, first):
                act.wait_ge(v_in[b], (i + 1) * 16)
                if not first:
                    act.wait_ge(pe_y, i * RB + (b - 1))
                nc.scalar.copy(hi[:, b % 2, 1, :], raw[:, b, 1, :]).then_inc(v_hi, 1)

            def gelu(i, b, first):
                act.wait_ge(pe_h, i * RB + (b + 1))
                if not first:
                    act.wait_ge(a_lo, i * RB + (b - 1))
                nc.scalar.activation(gel[:, b % 2, :], ps[:, b % 2, 0:S], ACT.Gelu).then_inc(gelu_done, 1)

            for b in range(RB):
                u_split(0, b, b < 2)
                if b:
                    gelu(0, b - 1, b - 1 < 2)
                v_split(0, b, b < 2)
            with act.Fori(1, NK // RB) as i:
                for b in range(RB):
                    u_split(i, b, False)
                    gelu(i, b - 1, False)
                    v_split(i, b, False)
            gelu(NK // RB - 1, RB - 1, False)
            for t in range(T):
                norm(1, t)

        @block.vector
        def _(dve):
            v = nc.vector
            count = [0]

            def did(ins):
                count[0] += 1
                ins.then_inc(dve_chain, 1)

            def settle():
                dve.wait_ge(dve_chain, count[0])

            dve.wait_ge(l_const, 16)
            dve.wait_ge(l_pos, 16)
            did(v.tensor_copy(posf, pos_i[:, :]))
            settle()
            for t in range(T):
                did(v.tensor_scalar(ang[:, t, :], kc[:, K_FREQ:K_FREQ + 12], posf[:, t:t + 1], None, ALU.mult))
            settle()
            did(v.tensor_scalar(turns, ang, 1.0 / (2 * np.pi), MAGIC, ALU.mult, ALU.add))
            settle()
            did(v.tensor_scalar(turns, turns, -MAGIC, None, ALU.add))
            settle()
            for part in TWO_PI:
                did(v.scalar_tensor_tensor(out=ang, in0=turns, scalar=-part, in1=ang, op0=ALU.mult, op1=ALU.add))
                settle()
            did(v.tensor_scalar(turns, ang, PI_IN, -PI_IN, ALU.min, ALU.max))
            did(v.tensor_scalar(sinv, ang, float(np.float32(np.pi / 2)), None, ALU.is_gt))
            settle()
            did(v.tensor_scalar(ang, ang, float(np.float32(np.pi / 2)), None, ALU.add))
            settle()
            did(v.scalar_tensor_tensor(out=ang, in0=sinv, scalar=float(np.float32(-2 * np.pi)), in1=ang,
                                       op0=ALU.mult, op1=ALU.add))
            settle()
            did(v.tensor_scalar(ang, ang, PI_IN, -PI_IN, ALU.min, ALU.max))
            settle()
            v.tensor_scalar(turns, turns, 0.0, None, ALU.add).then_inc(ang_ready, 1)

            dve.wait_ge(trig, 2)
            for t in range(T):
                dve.wait_ge(h_saved, 4 * (t + 1))
                jobs = []
                for c0, heads, hd, f0, r0 in ((0, N64, HD, 0, 0), (C_IQ, N32, IDX_D, 8, 608)):
                    half = hd // 8
                    hv = h[:, t, c0:c0 + heads * hd].rearrange("p (h d) -> p h d", h=heads)
                    x1, x2 = hv[:, :, 0:half], hv[:, :, half:2 * half]
                    cs = cosv[:, t, f0:f0 + half].unsqueeze(1).to_broadcast([P, heads, half])
                    sn = sinv[:, t, f0:f0 + half].unsqueeze(1).to_broadcast([P, heads, half])
                    n = heads * half
                    tmp = [rt[:, r0 + m * n:r0 + (m + 1) * n].rearrange("p (h d) -> p h d", h=heads)
                           for m in range(4)]
                    did(v.tensor_tensor(tmp[0], x1, cs, ALU.mult))
                    did(v.tensor_tensor(tmp[1], x2, sn, ALU.mult))
                    did(v.tensor_tensor(tmp[2], x2, cs, ALU.mult))
                    did(v.tensor_tensor(tmp[3], x1, sn, ALU.mult))
                    jobs.append((x1, x2, tmp))
                settle()
                for x1, x2, tmp in jobs:
                    did(v.tensor_tensor(x1, tmp[0], tmp[1], ALU.subtract))
                    did(v.tensor_tensor(x2, tmp[2], tmp[3], ALU.add))
                settle()
                for d0, c0, g, n, w in ((0, C_KD, 1, 2, HD), (128, C_IK, 1, 4, IDX_D), (256, C_KC, 2, 2, HD),
                                        (512, C_VC, 2, 2, HD)):
                    for gg in range(g):
                        o = dup[:, t, d0 + gg * n * w:d0 + (gg + 1) * n * w].rearrange("p (n w) -> p n w", n=n)
                        did(v.tensor_copy(o, h[:, t, c0 + gg * w:c0 + (gg + 1) * w].unsqueeze(1)
                                          .to_broadcast([P, n, w])))
                did(v.tensor_scalar(iw[:, t, :], h[:, t, C_IW:C_IW + IDX_H], (IDX_H * IDX_D) ** -0.5, None, ALU.mult))
                settle()
                v.tensor_scalar(iw[:, t, :], iw[:, t, :], 0.0, None, ALU.add).then_inc(roped, 1)
                dve.wait_ge(gate_exp, t + 1)
                gt = gate[:, t, :, :].rearrange("p h b -> p (h b)")
                did(v.tensor_scalar(gt, gt, 1.0, None, ALU.add))
                settle()
                did(v.reciprocal(gt, gt))

            dve.wait_ge(pe_memp, 2)
            did(v.memset(ghv, 0.0))
            did(v.memset(vbd, 0.0))
            did(v.memset(pcp, 0.0))
            settle()
            v.memset(ghk, 0.0).then_inc(pad_zero, 1)

            dve.wait_ge(l_pe, 16)
            dve.wait_ge(tr_saved, 8)
            for a in range(2):
                s0 = KC if a == 0 else VC
                for g in range(2):
                    src = bass.AP(TT.tensor, TT[:, s0 + g, :].offset, [list(TT.ap[0]), [2, LP], [CMP_STRIDE, NC]])
                    ins = v.tensor_tensor(flat[:, a, :, g, :], src,
                                          pe_sb[:, a, :].unsqueeze(2).to_broadcast([P, LP, NC]), ALU.add)
                ins.then_inc(flat_ready, 1)

            dve.wait_ge(pe_kv, 1)
            did(v.tensor_copy(kcT[0:64, 0:NC], ps[0:64, 2, 0:NC]))
            v.tensor_copy(kcT[64:128, 0:NC], ps[64:128, 2, NC:2 * NC]).then_inc(kv_saved, 1)
            dve.wait_ge(pe_kv, 3)
            for g in range(2):
                for j in range(4):
                    r = slice(32 * j, 32 * j + 32)
                    ins = v.tensor_copy(vbd[r, g, j, :], ps[r, 3 + g, 0:HD])
                ins.then_inc(kv_saved, 1)

            for t in range(T):
                w = width(t, "idx")
                tri = kc[:, K_TRI + S - w:K_TRI + S]
                for i in range(IDX_H):
                    dve.wait_ge(relu_done, 8 * t + i + 1)
                    if i:
                        dve.wait_ge(idx_read, 8 * t + i)
                    v.scalar_tensor_tensor(out=score[:, t, 0:w], in0=rl[:, i // 4, i % 4, 0:w],
                                           scalar=iw[:, t, i:i + 1], in1=tri if i == 0 else score[:, t, 0:w],
                                           op0=ALU.mult, op1=ALU.add).then_inc(idx_read, 1)

            def index_round(t):
                w = width(t, "idx")
                did(v.max(top8, score[:, t, 0:w]))
                settle()
                did(v.match_replace(score[:, t, 0:w], top8, score[:, t, 0:w], TAKEN))
                settle()

            def index_bias(t):
                w = width(t, "idx")
                did(v.tensor_scalar(dbias[:, t, 0:w], score[:, t, 0:w], TAKEN, NEG, ALU.not_equal, ALU.mult))
                settle()
                did(v.tensor_tensor(dbias[:, t, 0:w], dbias[:, t, 0:w], kc[:, K_TRI + S - w:K_TRI + S], ALU.add))
                settle()

            def cmp_scores(t):
                dve.wait_ge(pe_cs, t + 1)
                if t:
                    dve.wait_ge(pe_cT, t)
                cb = kc[:, K_CB + t * NC:K_CB + (t + 1) * NC].unsqueeze(1).to_broadcast([P, 4, NC])
                for g in range(2):
                    did(v.tensor_tensor(pc[:, 4 * g:4 * g + 4, :],
                                        ps[:, 4 + g, 0:64].rearrange("p (j b) -> p j b", j=4)[:, :, 0:NC],
                                        cb, ALU.add))
                settle()
                did(v.tensor_reduce(cmax, pc, AX_X, ALU.max))
                settle()
                did(v.tensor_scalar(cmax, cmax, NEG / 10, None, ALU.max))
                settle()
                v.tensor_tensor(pc, pc, cmax.unsqueeze(2).to_broadcast([P, 8, NC]), ALU.subtract
                                ).then_inc(cx_ready, 1)

            def cmp_probs(t):
                dve.wait_ge(cx_exp, t + 1)
                did(v.tensor_reduce(cmax, pc, AX_X, ALU.add))
                settle()
                did(v.tensor_scalar(cmax, cmax, 1e-30, None, ALU.max))
                settle()
                did(v.reciprocal(cmax, cmax))
                settle()
                did(v.tensor_tensor(cmax, cmax, gate[:, t, :, 0], ALU.mult))
                settle()
                v.tensor_tensor(pcp[:, :, 0:NC], pc, cmax.unsqueeze(2).to_broadcast([P, 8, NC]), ALU.mult
                                ).then_inc(cp_ready, 1)

            def maxima(n):
                t, k, g = GROUPS[n]
                w = width(t, k)
                dve.wait_ge(pe_s, n + 1)
                if n >= 2:
                    dve.wait_ge(pe_pT, n - 1)
                for j in range(4):
                    pl = place(j)
                    c = 4 * (n % 2) + j
                    s = ps[:, 2 * (n % 2) + pl // 2, (pl % 2) * S:(pl % 2) * S + w]
                    if k == "mem":
                        did(v.tensor_reduce(gmax[:, c:c + 1], s, AX_X, ALU.max))
                    else:
                        bias = dbias[:, t, 0:w] if k == "dsa" else kc[:, K_TRI + S - w:K_TRI + S]
                        did(v.tensor_tensor_reduce(out=xb[:, n % 2, j, 0:w], in0=s, in1=bias, scale=1.0,
                                                   scalar=TAKEN, op0=ALU.add, op1=ALU.max,
                                                   accum_out=gmax[:, c:c + 1]))
                settle()
                c = slice(4 * (n % 2), 4 * (n % 2) + 4)
                v.tensor_scalar(gneg[:, c], gmax[:, c], -SCALE, None, ALU.mult).then_inc(neg_ready, 1)

            def normalise(n):
                t, k, g = GROUPS[n]
                w = width(t, k)
                c = slice(4 * (n % 2), 4 * (n % 2) + 4)
                dve.wait_ge(exp_done, 4 * (n + 1))
                did(v.reciprocal(grec[:, c], gden[:, c]))
                settle()
                if k in ("sel", "win"):
                    did(v.tensor_tensor(grec[:, c], grec[:, c],
                                        gate[:, t, 4 * g:4 * g + 4, 1 if k == "sel" else 2], ALU.mult))
                    settle()
                for j in range(4):
                    ins = v.tensor_scalar(xb[:, n % 2, j, 0:w], xb[:, n % 2, j, 0:w],
                                          grec[:, 4 * (n % 2) + j:4 * (n % 2) + j + 1], None, ALU.mult)
                ins.then_inc(prob_ready, 1)

            for t in range(T):
                n0 = t * len(KINDS)
                cmp_scores(t)
                if t == 0:
                    maxima(0)
                cmp_probs(t)
                dve.wait_ge(idx_read, 8 * (t + 1))
                for n in range(n0, n0 + len(KINDS)):
                    normalise(n)
                    if n + 1 < len(GROUPS):
                        maxima(n + 1)
                    if n < n0 + 4:
                        for _ in range(TOPK_DSA // 8 // 4):
                            index_round(t)
                    if n == n0 + 3:
                        index_bias(t)

            def norm(n, t, param):
                st = lnst[:, t, :]
                did(v.scalar_tensor_tensor(out=xs[:, t, :], in0=xs[:, t, :], scalar=ALPHA, in1=bank2(2 + t),
                                           op0=ALU.mult, op1=ALU.add, accum_out=st[:, 0:1]))
                settle()
                did(v.tensor_scalar(st[:, 1:2], st[:, 0:1], 1.0 / D, None, ALU.mult))
                settle()
                v.tensor_scalar(xs[:, t, :], xs[:, t, :], st[:, 1:2], None, ALU.subtract).then_inc(centred, 1)
                dve.wait_ge(squared, n * T + t + 1)
                v.tensor_scalar(st[:, 3:4], st[:, 2:3], 1.0 / D, EPS, ALU.mult, ALU.add).then_inc(var_ready, 1)
                dve.wait_ge(rooted, n * T + t + 1)
                did(v.reciprocal(st[:, 5:6], st[:, 4:5]))
                settle()
                did(v.scalar_tensor_tensor(out=xs[:, t, :], in0=xs[:, t, :], scalar=st[:, 5:6], in1=param[:, 0, :],
                                           op0=ALU.mult, op1=ALU.mult))
                settle()
                v.tensor_tensor(xs[:, t, :], xs[:, t, :], param[:, 1, :], ALU.add
                                ).then_inc(x1_ready if n == 0 else y_ready, 1)

            dve.wait_ge(l_x, 16)
            dve.wait_ge(l_ln1, 16)
            for t in range(T):
                dve.wait_ge(pe_mix, t + 1)
                norm(0, t, ln_sb)

            dve.wait_ge(xT_saved, T)
            v.tensor_copy(x1hl[:, :, 0, :], x1T).then_inc(x1_split, 1)
            dve.wait_ge(x1_split, 1)
            v.tensor_tensor(x1hl[:, :, 1, :], x1T, x1hl[:, :, 0, :].bitcast(F32), ALU.subtract).then_inc(x1_split, 1)

            def top16(jobs):
                for o in (0, 8):
                    for vals, _, s in jobs:
                        did(v.max(vals[:, o:o + 8], s))
                    settle()
                    for vals, idx, s in jobs:
                        did(v.max_index(idx[:, o:o + 8], vals[:, o:o + 8], s))
                    if o == 0:
                        settle()
                        for vals, _, s in jobs:
                            did(v.match_replace(s, vals[:, 0:8], s, TAKEN))
                    settle()

            for b in range(2 * PH):
                dve.wait_ge(sk_saved, b + 1)
                top16([(V[:, t, b, :], IX[:, t, b, :], sc[:, t, b, :]) for t in range(T)])

            for t in range(T):
                did(v.tensor_copy(IF, IX[:, t, :, :]))
                settle()
                i1 = IF.rearrange("p (h a) k -> p h a k", a=2)[:, :, 0, :]
                i2 = IF.rearrange("p (h a) k -> p h a k", a=2)[:, :, 1, :]
                v1 = V[:, t, :, :].rearrange("p (h a) k -> p h a k", a=2)[:, :, 0, :]
                v2 = V[:, t, :, :].rearrange("p (h a) k -> p h a k", a=2)[:, :, 1, :]
                did(v.tensor_scalar(i1, i1, float(NK), None, ALU.mult))
                settle()
                for r0, r, c in RUNS:
                    sl = slice(OFF[r0], OFF[r0] + r * c)
                    for o, a1, a2 in ((cand, v1, v2), (cande, i1, i2)):
                        did(v.tensor_tensor(o[:, :, sl].rearrange("p h (r c) -> p h r c", r=r),
                                            a1[:, :, r0:r0 + r].unsqueeze(3).to_broadcast([P, PH, r, c]),
                                            a2[:, :, 0:c].unsqueeze(2).to_broadcast([P, PH, r, c]), ALU.add))
                settle()
                top16([(tv[:, hh, :], ti[:, hh, :], cand[:, hh, :]) for hh in range(PH)])
                v.tensor_tensor(te, tv, tv[:, :, 0:1].to_broadcast([P, PH, TK]), ALU.subtract).then_inc(g_shift, 1)
                did(v.tensor_copy(tf, ti))
                settle()
                eqv = eq.rearrange("p (m c) -> p m c", c=NCAND)
                did(v.tensor_tensor(eqv, tf.rearrange("p h k -> p (h k)").unsqueeze(2).to_broadcast([P, PH * TK, NCAND]),
                                    kc[:, K_IOTA:K_IOTA + NCAND].unsqueeze(1).to_broadcast([P, PH * TK, NCAND]),
                                    ALU.is_equal))
                settle()
                eqh = eq.rearrange("p (h k c) -> p h k c", h=PH, k=TK)
                did(v.tensor_tensor(eqh, eqh, cande.unsqueeze(2).to_broadcast([P, PH, TK, NCAND]), ALU.mult))
                if t:
                    dve.wait_ge(pe_rT, t)
                settle()
                tfl = tf.rearrange("p h k -> p (h k)")
                did(v.tensor_reduce(tfl, eqv, AX_X, ALU.add))
                settle()
                did(v.tensor_scalar(ex[:, 0, :], tfl, 1.0 / NK, -(NK - 1) / (2.0 * NK), ALU.mult, ALU.add))
                settle()
                did(v.tensor_scalar(ex[:, 0, :], ex[:, 0, :], MAGIC, None, ALU.add))
                settle()
                did(v.tensor_scalar(ex[:, 0, :], ex[:, 0, :], -MAGIC, None, ALU.add))
                settle()
                did(v.scalar_tensor_tensor(out=ex[:, 1, :], in0=ex[:, 0, :], scalar=-float(NK), in1=tfl,
                                           op0=ALU.mult, op1=ALU.add))
                dve.wait_ge(g_exp, t + 1)
                did(v.tensor_reduce(gs[:, 0:PH], te, AX_X, ALU.add))
                settle()
                did(v.reciprocal(gs[:, PH:2 * PH], gs[:, 0:PH]))
                settle()
                v.tensor_tensor(ex[:, 2, :].rearrange("p (h k) -> p h k", h=PH), te,
                                gs[:, PH:2 * PH].unsqueeze(2).to_broadcast([P, PH, TK]), ALU.mult
                                ).then_inc(route_ready, 1)

            def onehots(i, first):
                for b in range(2):
                    if not first:
                        dve.wait_ge(pe_g, i * 2 + (b - 1))
                    for q in range(4):
                        tok = bass.ds(i * 8 + (b * 4 + q), 1)
                        if q >= POOL_HOT:
                            v.tensor_scalar(oh[:, b, 0, q, :], iota, slotT[:, 1, tok], None, ALU.is_equal)
                        ins = v.tensor_scalar(oh[:, b, 1, q, :], iota, slotT[:, 0, tok], slotT[:, 2, tok],
                                              ALU.is_equal, ALU.mult)
                    ins.then_inc(oh_ready, 1)

            dve.wait_ge(rT_saved, T)
            onehots(0, True)
            with dve.Fori(1, S // 8) as i:
                onehots(i, False)

            def u_rest(i, b):
                dve.wait_ge(u_hi, i * RB + (b + 1))
                v.tensor_tensor(lo[:, b, 0, :], raw[:, b, 0, :], hi[:, b % 2, 0, :].bitcast(F32),
                                ALU.subtract).then_inc(u_lo, 1)

            def v_rest(i, b):
                dve.wait_ge(v_hi, i * RB + (b + 1))
                v.tensor_tensor(lo[:, b, 1, :], raw[:, b, 1, :], hi[:, b % 2, 1, :].bitcast(F32),
                                ALU.subtract).then_inc(v_lo, 1)

            def a_split(i, b, first):
                dve.wait_ge(gated, i * RB + (b + 1))
                if not first:
                    dve.wait_ge(pe_y, i * RB + (b - 1))
                v.tensor_copy(ahl[:, b % 2, 0, :], gel[:, b % 2, :]).then_inc(a_hi, 1)
                dve.wait_ge(a_hi, i * RB + (b + 1))
                v.tensor_tensor(ahl[:, b % 2, 1, :], gel[:, b % 2, :], ahl[:, b % 2, 0, :].bitcast(F32),
                                ALU.subtract).then_inc(a_lo, 1)

            for b in range(RB):
                u_rest(0, b)
                if b:
                    a_split(0, b - 1, b - 1 < 2)
                v_rest(0, b)
            with dve.Fori(1, NK // RB) as i:
                for b in range(RB):
                    u_rest(i, b)
                    a_split(i, b - 1, False)
                    v_rest(i, b)
            a_split(NK // RB - 1, RB - 1, False)

            dve.wait_ge(l_ln2, 16)
            dve.wait_ge(pe_y, NK)
            for t in range(T):
                norm(1, t, ln2_sb)


def kernel(**inputs):
    import concourse.bacc as _bacc
    from concourse.bass_utils import run_bass_kernel_spmd as _run

    a = {k: np.ascontiguousarray(v) for k, v in inputs.items()}

    def rows(w):
        return np.ascontiguousarray(w.reshape(-1, P, w.shape[-1]).transpose(1, 0, 2))

    w = a["w_in"][0]
    ends = np.cumsum([512, 768, 24, 256, 128, 256, 32, 8, 256])
    nq, kv, gt, dq, dkv, iq, ik, iwt, mqw = np.split(w, ends[:-1], axis=1)
    nq = nq.reshape(D, 2, 4, HD).transpose(0, 2, 1, 3).reshape(D, 512)
    kv = kv.reshape(D, 6, 128)
    tok = np.concatenate([nq, kv[:, 0], kv[:, 2], kv[:, 4], dq, dkv[:, :HD], iq, ik,
                          kv[:, 1], kv[:, 3], kv[:, 5], dkv[:, HD:], gt, iwt], axis=1)
    wm = a["w_mem_kv"][0]
    wq = a["peer_w_query"][0]
    w2k = a["nsa_cmp_w2_k"][0]

    def pe_rows(m):
        return m.reshape(LP, P).T

    arrays = {
        "x": rows(a["x"][0]), "xT": rows(a["x"][0].T), "memT": rows(a["mem"][0].T),
        "positions": np.ascontiguousarray(a["positions"][0].reshape(T, P).T),
        "w_tok": rows(tok), "w_memq": rows(mqw), "w_memk": rows(wm[:, :256]), "w_memv": rows(wm[:, 256:]),
        "w1k": rows(a["nsa_cmp_w1_k"][0]), "w1v": rows(a["nsa_cmp_w1_v"][0]),
        "w2k": np.concatenate([w2k, w2k], axis=1), "w2v": a["nsa_cmp_w2_v"][0],
        "peT": np.ascontiguousarray(np.stack([pe_rows(a["nsa_pe_k"][0]), pe_rows(a["nsa_pe_v"][0])], axis=1)),
        "w_out": rows(a["w_out"][0]), "ln1": np.stack([a["ln1_g"][0], a["ln1_b"][0]]),
        "wqa": rows(wq[:, :1024]), "wqb": rows(wq[:, 1024:]),
        "subk": np.ascontiguousarray(np.stack([a["peer_sub_keys_1"][0].T, a["peer_sub_keys_2"][0].T], axis=1)),
        "uT": np.ascontiguousarray(a["peer_u"][0].reshape(NK, P, KD, P).transpose(0, 3, 2, 1)).reshape(NK, P, D),
        "pv": a["peer_v"][0].reshape(NK, P, D),
        "ln2": np.stack([a["ln2_g"][0], a["ln2_b"][0]]),
        "consts": constants(),
    }
    nc = _bacc.Bacc("TRN2", target_bir_lowering=False, num_devices=1)
    args = {n: nc.dram_tensor(f"in_{n}", list(v.shape), mybir.dt.from_np(v.dtype), kind="ExternalInput").ap()
            for n, v in arrays.items()}
    out = nc.dram_tensor("out", [S, D], F32, kind="ExternalOutput").ap()
    peer_layer_kernel(nc, out=out, **args)
    r = _run(nc, [{f"in_{n}": np.ascontiguousarray(v) for n, v in arrays.items()}], core_ids=[0])
    return r.results[0]["out"].reshape(1, S, D)
```

```python
from contextlib import ExitStack

import numpy as np
import concourse.bass as bass
import concourse.mybir as mybir

F32 = mybir.dt.float32
F32R = mybir.dt.float32r
I32 = mybir.dt.int32
U32 = mybir.dt.uint32
ALU = mybir.AluOpType
ACT = mybir.ActivationFunctionType
AX_X = mybir.AxisListType.X

P = 128
D = 1024
S = 256
T = S // P
KD = D // P
HD = 64
SCALE = HD ** -0.5
CMP_LEN, CMP_STRIDE = 32, 16
NC = (S - CMP_LEN) // CMP_STRIDE + 1
LP = CMP_LEN * HD // P
MEM = 256
TOPK_DSA = min(256, S // 4)
IDX_H, IDX_D = 8, 32
PH = 8
NK = 128
TK = 16
ALPHA = 2.0 ** 0.25
EPS = 1e-5
NEG = -1e38
TAKEN = -3e38
TWO_PI = (6.28125, 0.0019350051879882812, 2 * np.pi - 6.28125 - 0.0019350051879882812)
PI_IN = 3.1415925
NPRE = 24
POOL_HOT = 2
OB = 4
GN = S // 4
RB = 4
NP = NPRE // RB
NM = NK // RB - NP
MAGIC = 1.5 * 2 ** 23

C_NQ, C_KC, C_KS, C_KW, C_DQ, C_KD = 0, 512, 640, 768, 896, 1152
C_IQ, C_IK = 1216, 1472
C_VC, C_VS, C_VW, C_VD, C_GATE, C_IW = 1504, 1632, 1760, 1888, 1952, 1976
C_ALL = 1984
N64 = 19
N32 = 9
CHUNKS = [(0, 512), (512, 512), (1024, 512), (1536, C_ALL - 1536)]

NQ, KS, KW, DQ, KDD, IQ, IK, KC, VC = 0, 4, 5, 6, 8, 9, 11, 12, 14
SLOTS = 16

COUNT = [TK // (i + 1) for i in range(TK)]
OFF = [sum(COUNT[:i]) for i in range(TK)]
NCAND = sum(COUNT)
RUNS = []
for _i in range(TK):
    if RUNS and RUNS[-1][2] == COUNT[_i]:
        RUNS[-1] = (RUNS[-1][0], RUNS[-1][1] + 1, COUNT[_i])
    else:
        RUNS.append((_i, 1, COUNT[_i]))

K_ID, K_IOTA, K_TRI, K_CB, K_FREQ = 0, 128, 256, 512, 512 + T * NC
K_ALL = K_FREQ + 12


def constants():
    c = np.zeros((P, K_ALL), np.float32)
    c[:, K_ID:K_ID + P] = np.eye(P, dtype=np.float32)
    c[:, K_IOTA:K_IOTA + P] = np.arange(P, dtype=np.float32)
    row = np.arange(P)[:, None]
    c[:, K_TRI + P:K_TRI + 2 * P] = np.where(np.arange(P)[None, :] <= row, 0.0, NEG)
    for t in range(T):
        end = np.arange(NC)[None, :] * CMP_STRIDE + CMP_LEN - 1
        c[:, K_CB + t * NC:K_CB + (t + 1) * NC] = np.where(end <= row + t * P, 0.0, NEG)
    for at, half in ((0, 8), (8, 4)):
        c[:, K_FREQ + at:K_FREQ + at + half] = (500000.0 ** (-np.arange(half) / half)).astype(np.float32)
    return c


A_WIN = 0
A_WQA = 0
A_TT = 8192
A_X = A_TT + SLOTS * S
A_PT = A_X + 2 * 1024
A_END1 = A_PT + 2 * 1024
A_OT = A_TT
A_WQB = 8192
A_XT = 16384
A_S = A_XT + 2048
A_WOUT = KD * (C_ALL + 256)
A_H = A_WOUT + KD * D
A_MQ = A_H + T * C_ALL
A_RT = A_MQ + 1536
A_QT = A_S + 4096
A_V = A_QT + 512
A_I = A_V + 512
A_R = A_I + 512
A_ALL = 32768


def peer_layer_kernel(nc, x, xT, memT, positions, w_tok, w_memq, w_memk, w_memv, w1k, w1v, w2k, w2v, peT,
                      w_out, ln1, wqa, wqb, subk, uT, pv, ln2, consts, out):
    with ExitStack() as ctx:
        def sb(name, shape, dt=F32):
            return ctx.enter_context(nc.sbuf_tensor(name, shape, dt))

        def sem(name):
            return ctx.enter_context(nc.semaphore(name))

        arena = sb("arena", [P, A_ALL])
        slab_at = nc.sbuf_base
        slab = sb("slab", [P, 4 * 4096 + 128])
        raw = slab[:, 0:8192].rearrange("p (b a n) -> p b a n", b=RB, a=2)
        lo = nc.alloc_sbuf_tensor_at("lo", [P, RB, 2, 1024], F32R, offset=slab_at)
        hi = nc.alloc_sbuf_tensor_at("hi", [P, 2, 2, 1024], F32R, offset=slab_at + 4 * 8320)
        x1hl = nc.alloc_sbuf_tensor_at("x1hl", [P, KD, 2, S], F32R, offset=slab_at + 4 * 12416)
        xs = sb("xs", [P, T, D])
        ahl = sb("ahl", [P, 2, 2, S], F32R)
        gel = sb("gel", [P, 2, S])
        oh = slab[:, 4096:6144].rearrange("p (b a q n) -> p b a q n", b=2, a=2, q=4)
        kc = slab[:, 6144:6144 + K_ALL]
        sm = slab[:, 6144 + K_ALL:8320]
        n2 = sb("n2", [P, OB, 4])
        lnst = sb("lnst", [P, T, 8])
        pos_i = sb("pos_i", [P, T], I32)
        ps = ctx.enter_context(nc.psum_tensor("ps", [P, 8, 512], F32))

        def ar(at, n):
            return arena[:, at:at + n]

        ident = kc[:, K_ID:K_ID + P]
        iota = kc[:, K_IOTA:K_IOTA + P]

        at = [0]

        def small(n):
            at[0] += n
            assert at[0] <= 8320 - 6144 - K_ALL
            return sm[:, at[0] - n:at[0]]

        posf = small(T)
        ang = small(T * 12).rearrange("p (t f) -> p t f", t=T)
        turns = small(T * 12).rearrange("p (t f) -> p t f", t=T)
        cosv = small(T * 12).rearrange("p (t f) -> p t f", t=T)
        sinv = small(T * 12).rearrange("p (t f) -> p t f", t=T)
        gate = small(T * 24).rearrange("p (t h b) -> p t h b", t=T, b=3)
        iw = small(T * 8).rearrange("p (t h) -> p t h", t=T)
        kcT = small(16)
        cmax = small(8)
        gmax = small(16)
        gneg = small(16)
        gden = small(16)
        grec = small(16)
        gcoef = small(16)
        slotT = small(3 * S).rearrange("p (a t) -> p a t", a=3)
        pe_sb = small(2 * LP).rearrange("p (a l) -> p a l", a=2)
        w2k_sb = oh[:, 1, 1, 0, :]
        w2v_sb = oh[:, 1, 1, 1, 0:HD]
        subk_sb = small(2 * P).rearrange("p (a n) -> p a n", a=2)

        dup = oh[:, :, :, :, :].rearrange("p a b c d -> p (a b c d)")[:, 0:1536].rearrange(
            "p (t n) -> p t n", t=T)
        w_t = ar(A_WIN, KD * C_ALL).rearrange("p (k n) -> p k n", k=KD)
        w_mq = ar(A_WIN + KD * C_ALL, KD * 256).rearrange("p (k n) -> p k n", k=KD)
        w_o = ar(A_WOUT, KD * D).rearrange("p (k n) -> p k n", k=KD)
        h = ar(A_H, T * C_ALL).rearrange("p (t n) -> p t n", t=T)
        mq = ar(A_MQ, 1536).rearrange("p (a b s) -> p a b s", a=3, b=2)
        rawf = slab[:, 0:4096]
        w_mk = rawf[:, 0:2048].rearrange("p (k n) -> p k n", k=KD)
        w_mv = rawf[:, 2048:4096].rearrange("p (k n) -> p k n", k=KD)
        xhf = slab[:, 12416:16512]
        memT_sb = xhf[:, 0:2048].rearrange("p (k n) -> p k n", k=KD)
        xT_sb = xhf[:, 2048:4096].rearrange("p (k n) -> p k n", k=KD)
        hif = slab[:, 8320:12416]
        w1 = hif[:, 0:4096].rearrange("p (a l n) -> p a l n", a=2, l=LP)
        ln_sb = hif[:, 0:2048].rearrange("p (a n) -> p a n", a=2)
        rt = ar(A_RT, 1120)
        TT = ar(A_TT, SLOTS * S).rearrange("p (s t) -> p s t", s=SLOTS)
        xb = ar(A_X, 2048).rearrange("p (b j n) -> p b j n", b=2, j=4)
        PT = ar(A_PT, 2048).rearrange("p (b j n) -> p b j n", b=2, j=4)
        oT = ar(A_OT, 2048).rearrange("p (k t) -> p k t", k=KD)
        ocs = [oh[:, 1 - t, :, :, :].rearrange("p a b c -> p (a b c)") for t in range(T)]
        flat = ar(A_RT, 960).rearrange("p (a l g b) -> p a l g b", a=2, l=LP, g=2)
        CX = A_END1
        assert CX + 1536 <= A_WOUT
        ghk = ar(CX, 32)
        ghv = ar(CX + 32, 256).rearrange("p (g j b) -> p g j b", g=2, j=4)
        vbd = ar(CX + 288, 512).rearrange("p (g j n) -> p g j n", g=2, j=4)
        pc = ar(CX + 800, 120).rearrange("p (h b) -> p h b", h=8)
        pcp = ar(CX + 920, 256).rearrange("p (h b) -> p h b", h=8)
        score = oh[:, 0, 0, :, :].rearrange("p a b -> p (a b)").rearrange("p (t s) -> p t s", t=T)
        dbias = oh[:, 0, 1, :, :].rearrange("p a b -> p (a b)").rearrange("p (t s) -> p t s", t=T)
        rl = PT
        pcT = ar(CX + 1176, 256).rearrange("p (g t) -> p g t", g=2)
        top8 = gcoef[:, 0:8]

        x1T = ar(A_XT, 2048).rearrange("p (k t) -> p k t", k=KD)
        wq_sb = [ar(A_WQA, 8192).rearrange("p (k n) -> p k n", k=KD),
                 ar(A_WQB, 8192).rearrange("p (k n) -> p k n", k=KD)]
        sc = ar(A_S, 4096).rearrange("p (t b n) -> p t b n", t=T, b=2 * PH)
        qT = ar(A_QT, 512).rearrange("p (b t) -> p b t", b=2)
        V = ar(A_V, 512).rearrange("p (t b k) -> p t b k", t=T, b=2 * PH)
        IX = ar(A_I, 512).bitcast(U32).rearrange("p (t b k) -> p t b k", t=T, b=2 * PH)
        IF = ar(A_R, 256).rearrange("p (b k) -> p b k", b=2 * PH)
        cand = ar(A_R + 256, PH * NCAND).rearrange("p (h c) -> p h c", h=PH)
        cande = ar(A_R + 656, PH * NCAND).rearrange("p (h c) -> p h c", h=PH)
        tv = ar(A_R + 1056, 128).rearrange("p (h k) -> p h k", h=PH)
        ti = ar(A_R + 1184, 128).bitcast(U32).rearrange("p (h k) -> p h k", h=PH)
        junk = ar(A_H, 2048).rearrange("p (t n) -> p t n", t=T)
        tf = ar(A_R + 1312, 128).rearrange("p (h k) -> p h k", h=PH)
        ex = ar(A_S, 768).rearrange("p (t a s) -> p t a s", t=T, a=3)
        te = ar(A_S + 768, 256).rearrange("p (t h k) -> p t h k", t=T, h=PH)
        gs = ar(A_R + 1952, 16)
        eq = ar(A_R + 1968, PH * TK * NCAND)
        assert A_R + 1968 + PH * TK * NCAND <= A_ALL
        G = arena[:, :].rearrange("p (c t) -> p c t", c=NK)
        ln2_sb = ar(0, 2048).rearrange("p (a n) -> p a n", a=2)

        l_const, l_pos, l_pe, l_x = sem("l_const"), sem("l_pos"), sem("l_pe"), sem("l_x")
        l_xT, l_mT, l_wmk, l_wmv, l_wmq = (sem(n) for n in ("l_xT", "l_mT", "l_wmk", "l_wmv", "l_wmq"))
        l_w = [sem(f"l_wtok{n}") for n in range(len(CHUNKS))]
        l_first = [sem(f"l_first{k}") for k in range(KD // 2)]
        l_w1, l_w2, l_wo, l_ln1 = sem("l_w1"), sem("l_w2"), sem("l_wo"), sem("l_ln1")
        l_wqa, l_wqb, l_sk, l_ln2 = sem("l_wqa"), sem("l_wqb"), sem("l_sk"), sem("l_ln2")
        pe_proj, h_saved = sem("pe_proj"), sem("h_saved")
        pe_memp, mem_saved = sem("pe_memp"), sem("mem_saved")
        dve_chain = sem("dve_chain")
        ang_ready, trig = sem("ang_ready"), sem("trig")
        roped = sem("roped")
        gate_exp = sem("gate_exp")
        pe_tr, tr_saved = sem("pe_tr"), sem("tr_saved")
        flat_ready, pe_hid, hid_act = sem("flat_ready"), sem("pe_hid"), sem("hid_act")
        pad_zero, pe_kv, kv_saved = sem("pad_zero"), sem("pe_kv"), sem("kv_saved")
        pe_idx, relu_done, idx_read = sem("pe_idx"), sem("relu_done"), sem("idx_read")
        pe_cs, cx_ready, cx_exp, cp_ready = sem("pe_cs"), sem("cx_ready"), sem("cx_exp"), sem("cp_ready")
        pe_cT, cT_saved = sem("pe_cT"), sem("cT_saved")
        pe_s, neg_ready, exp_done, prob_ready = sem("pe_s"), sem("neg_ready"), sem("exp_done"), sem("prob_ready")
        pe_pT, pT_saved, pe_pv = sem("pe_pT"), sem("pT_saved"), sem("pe_pv")
        o_saved, pe_oT, oT_saved, pe_mix = sem("o_saved"), sem("pe_oT"), sem("oT_saved"), sem("pe_mix")
        centred, squared, var_ready, rooted = sem("centred"), sem("squared"), sem("var_ready"), sem("rooted")
        x1_ready, pe_xT, xT_saved, x1_split = sem("x1_ready"), sem("pe_xT"), sem("xT_saved"), sem("x1_split")
        pe_q, q_saved, pe_sk, sk_saved = sem("pe_q"), sem("q_saved"), sem("pe_sk"), sem("sk_saved")
        g_shift, g_exp, route_ready = sem("g_shift"), sem("g_exp"), sem("route_ready")
        pe_rT, rT_saved = sem("pe_rT"), sem("rT_saved")
        n2_ready, n2_seen, oh2_ready = sem("n2_ready"), sem("n2_seen"), sem("oh2_ready")
        hot_dist, oh3_ready = sem("hot_dist"), sem("oh3_ready")
        oh_ready, pe_g, g_saved = sem("oh_ready"), sem("pe_g"), sem("g_saved")
        pu_in = [sem(f"pu_in{b}") for b in range(RB)]
        pu_hi, pu_lo, pe_ph, pre_gelu, pre_gated = (sem(n) for n in ("pu_hi", "pu_lo", "pe_ph", "pre_gelu", "pre_gated"))
        u_in = [sem(f"u_in{b}") for b in range(RB)]
        v_in = [sem(f"v_in{b}") for b in range(RB)]
        u_hi, u_lo, v_hi, v_lo = sem("u_hi"), sem("u_lo"), sem("v_hi"), sem("v_lo")
        pe_h, gelu_done, gated, a_hi, a_lo, pe_y = (sem(n) for n in ("pe_h", "gelu_done", "gated", "a_hi", "a_lo", "pe_y"))
        y_ready, stored = sem("y_ready"), sem("stored")

        KINDS = [("sel", 0), ("sel", 1), ("win", 0), ("win", 1), ("mem", 0), ("dsa", 0)]
        GROUPS = [(t, k, g) for t in range(T) for k, g in KINDS]

        def width(t, k):
            return MEM if k == "mem" else P * (t + 1)

        def place(j):
            return (j % 2) * 2 + j // 2

        def bank2(b):
            return ps[:, 2 * b:2 * b + 2, :].rearrange("p a n -> p (a n)")

        def hot(b):
            if b < 2:
                return oh[:, b]
            return raw[:, b - 2, 0, :].rearrange("p (a q n) -> p a q n", a=2, q=4)

        def gate_bank(b):
            return (2, 3, 6, 7)[b]

        def pre(buffers, b):
            return buffers[:, b // 2, b % 2, :]

        block = ctx.enter_context(nc.Block())

        @block.sync
        def _(sp):
            sp.dma_start(xT_sb, xT).then_inc(l_xT, 16)
            for k in range(0, KD, 2):
                sp.dma_start(w_t[:, k:k + 2, 0:512], w_tok[:, k:k + 2, 0:512]).then_inc(l_first[k // 2], 16)
            for n, (c0, w) in list(enumerate(CHUNKS))[1:]:
                sp.dma_start(w_t[:, :, c0:c0 + w], w_tok[:, :, c0:c0 + w]).then_inc(l_w[n], 16)
            sp.dma_start(w_mq, w_memq).then_inc(l_wmq, 16)
            sp.dma_start(memT_sb, memT).then_inc(l_mT, 16)
            sp.dma_start(w_mk, w_memk).then_inc(l_wmk, 16)
            sp.dma_start(w_mv, w_memv).then_inc(l_wmv, 16)
            sp.dma_start(w1[:, 0], w1k).then_inc(l_w1, 16)
            sp.dma_start(w1[:, 1], w1v).then_inc(l_w1, 16)
            sp.dma_start(w_o, w_out).then_inc(l_wo, 16)
            sp.wait_ge(pe_proj, T * len(CHUNKS))
            sp.dma_start(wq_sb[0], wqa).then_inc(l_wqa, 16)
            sp.wait_ge(pe_hid, 2)
            sp.dma_start(ln_sb, ln1.partition_broadcast(P)).then_inc(l_ln1, 16)
            sp.wait_ge(pe_mix, 2)
            sp.dma_start(wq_sb[1], wqb).then_inc(l_wqb, 16)
            sp.wait_ge(pe_memp, 6)

            def load_pre(i, first):
                for b in range(RB):
                    if not first:
                        sp.wait_ge(pe_ph, i * RB + (b - RB + 1))
                    sp.dma_start(pre(raw, b), uT[bass.ds(i * RB + b, 1)].rearrange("o p n -> (o p) n")
                                 ).then_inc(pu_in[b], 16)

            def load_u(j, b, first):
                if not first:
                    sp.wait_ge(pe_h, j * RB + (b - RB + 1))
                sp.dma_start(raw[:, b, 0, :], uT[bass.ds(j * RB + (NPRE + b), 1)].rearrange("o p n -> (o p) n")
                             ).then_inc(u_in[b], 16)

            def load_v(i, b, first):
                if not first:
                    sp.wait_ge(pe_y, i * RB + (b - RB + 1))
                sp.dma_start(raw[:, b, 1, :], pv[bass.ds(i * RB + b, 1)].rearrange("o p n -> (o p) n")
                             ).then_inc(v_in[b], 16)

            load_pre(0, True)
            with sp.Fori(1, NP) as i:
                load_pre(i, False)
            sp.wait_ge(pe_ph, NPRE)
            load_v(0, 0, True)
            load_v(0, 1, True)
            sp.wait_ge(pe_g, GN)
            load_v(0, 2, True)
            load_v(0, 3, True)
            for b in range(RB):
                load_u(0, b, True)
            with sp.Fori(1, NP + 1) as i:
                for b in range(RB):
                    load_v(i, b, False)
            with sp.Fori(1, NM) as j:
                for b in range(RB):
                    load_u(j, b, False)
                    load_v(j + NP, b, False)
            for t in range(T):
                sp.wait_ge(y_ready, t + 1)
                sp.dma_start(out[t * P:(t + 1) * P, :], xs[:, t, :]).then_inc(stored, 16)
            sp.wait_ge(stored, 16 * T)

        @block.gpsimd
        def _(pool):
            pool.dma_start(kc[:, :], consts).then_inc(l_const, 16)
            pool.dma_start(pos_i[:, :], positions).then_inc(l_pos, 16)
            pool.dma_start(pe_sb, peT).then_inc(l_pe, 16)
            pool.dma_start(w2k_sb, w2k).then_inc(l_w2, 16)
            pool.dma_start(w2v_sb, w2v).then_inc(l_w2, 16)
            pool.dma_start(subk_sb, subk).then_inc(l_sk, 16)
            pool.dma_start(xs[:, :, :], x).then_inc(l_x, 16)

            def chunk(i):
                for b in range(2):
                    pool.wait_ge(gelu_done, i * 2 + (b + 1))
                    nc.gpsimd.tensor_tensor(out=gel[:, b, :], in0=gel[:, b, :],
                                            in1=G[:, bass.ds(i * 2 + (NPRE + b), 1), :].rearrange("p o t -> p (o t)"),
                                            op=ALU.mult).then_inc(gated, 1)

            with pool.Fori(0, NP) as i:
                for b in range(RB):
                    pool.wait_ge(pu_hi, i * RB + (b + 1))
                    nc.gpsimd.tensor_tensor(out=pre(lo, b), in0=pre(raw, b), in1=pre(hi, b).bitcast(F32),
                                            op=ALU.subtract).then_inc(pu_lo, 1)

            def onehots(i, first):
                for b in range(OB):
                    nc.gpsimd.tensor_copy(n2[:, b, :], slotT[:, 1, bass.ds(i * (4 * OB) + b * 4, 4)]
                                          ).then_inc(n2_ready, 1)
                    if not first:
                        pool.wait_ge(pe_g, i * OB + (b - OB + 1))
                    pool.wait_ge(n2_ready, i * OB + (b + 1))
                    pool.sem_inc(n2_seen, 1)
                    for q in range(POOL_HOT):
                        ins = nc.gpsimd.tensor_scalar(hot(b)[:, 0, q, :], iota, n2[:, b, q:q + 1], None, ALU.is_equal)
                    ins.then_inc(oh2_ready, 1)

            pool.wait_ge(rT_saved, T)
            onehots(0, True)
            with pool.Fori(1, GN // OB) as i:
                onehots(i, False)
            pool.wait_ge(g_saved, GN)
            with pool.Fori(0, (NK - NPRE) // 2) as i:
                chunk(i)
            pool.wait_ge(gated, NK - NPRE)
            pool.wait_ge(a_lo, NPRE)
            pool.dma_start(ln2_sb, ln2.partition_broadcast(P)).then_inc(l_ln2, 16)

        @block.tensor
        def _(pe):
            def mm(o, lhsT, rhs, start, stop):
                return nc.tensor.matmul(o, lhsT, rhs, start=start, stop=stop, skip_group_check=True)

            pe.wait_ge(l_xT, 16)
            for t in range(T):
                for n, (c0, w) in enumerate(CHUNKS):
                    if n:
                        pe.wait_ge(l_w[n], 16)
                    for k in range(KD):
                        if n == 0 and k % 2 == 0:
                            pe.wait_ge(l_first[k // 2], 16)
                        last = mm(ps[:, t * 4 + n, 0:w], xT_sb[:, k, t * P:(t + 1) * P], w_t[:, k, c0:c0 + w],
                                  k == 0, k == KD - 1)
                    last.then_inc(pe_proj, 1)

            pe.wait_ge(l_wmq, 16)
            pe.wait_ge(l_mT, 16)
            pe.wait_ge(l_wmk, 16)
            pe.wait_ge(l_wmv, 16)
            pe.wait_ge(h_saved, 6)
            for m in range(6):
                a, b = m // 2, m % 2
                for k in range(KD):
                    if a == 0:
                        ops = (w_mq[:, k, b * P:(b + 1) * P], xT_sb[:, k, :])
                    elif a == 1:
                        ops = (w_mk[:, k, b * P:(b + 1) * P], memT_sb[:, k, :])
                    else:
                        ops = (memT_sb[:, k, b * P:(b + 1) * P], w_mv[:, k, :])
                    last = mm(ps[:, m, 0:S], *ops, k == 0, k == KD - 1)
                last.then_inc(pe_memp, 1)

            src = ([("h", C_NQ + P * j) for j in range(4)] + [("h", C_KS), ("h", C_KW), ("h", C_DQ), ("h", C_DQ + P)]
                   + [("d", 0), ("h", C_IQ), ("h", C_IQ + P), ("d", 128)] + [("d", 256 + P * j) for j in range(4)])
            pe.wait_ge(h_saved, 8)
            pe.wait_ge(mem_saved, 6)
            pe.wait_ge(l_const, 16)
            for t in range(T):
                pe.wait_ge(roped, t + 1)
                for s, (kind, c0) in enumerate(src):
                    a = h[:, t, c0:c0 + P] if kind == "h" else dup[:, t, c0:c0 + P]
                    last = nc.tensor.transpose(ps[:, t * 4 + s // 4, (s % 4) * P:(s % 4 + 1) * P], a, ident)
                    if s % 4 == 3:
                        last.then_inc(pe_tr, 1)

            pe.wait_ge(l_w1, 32)
            pe.wait_ge(tr_saved, 8)
            for a in range(2):
                pe.wait_ge(flat_ready, a + 1)
                for l in range(LP):
                    last = mm(ps[:, a, 0:2 * NC], w1[:, a, l, :],
                              flat[:, a, l, :, :].rearrange("p g b -> p (g b)"), l == 0, l == LP - 1)
                last.then_inc(pe_hid, 1)
            pe.wait_ge(l_w2, 32)
            pe.wait_ge(hid_act, 3)
            mm(ps[:, 2, 0:2 * NC], w2k_sb, ghk[:, 0:2 * NC], True, True).then_inc(pe_kv, 1)
            for g in range(2):
                mm(ps[:, 3 + g, 0:HD], ghv[:, g, :, :].rearrange("p j b -> p (j b)"), w2v_sb,
                   True, True).then_inc(pe_kv, 1)

            pe.wait_ge(kv_saved, 3)
            for t in range(T):
                if t:
                    pe.wait_ge(relu_done, 8)
                w = width(t, "idx")
                for i in range(IDX_H):
                    r = slice(32 * (i % 4), 32 * (i % 4) + 32)
                    last = mm(ps[:, i % 4, (i // 4) * S:(i // 4) * S + w],
                              TT[r, IQ + i // 4, t * P:(t + 1) * P], TT[r, IK, 0:w], i < 4, True)
                last.then_inc(pe_idx, 1)

            def cmp_scores(t):
                for hh in range(8):
                    g, j = hh // 4, hh % 4
                    last = mm(ps[:, 4 + g, j * 16:j * 16 + NC], TT[64 * g:64 * g + 64, NQ + j, t * P:(t + 1) * P],
                              kcT[64 * g:64 * g + 64, 0:NC], j == 0, True)
                last.then_inc(pe_cs, 1)

            def cmp_out(t):
                pe.wait_ge(cp_ready, t + 1)
                for g in range(2):
                    last = nc.tensor.transpose(ps[:, 4 + g, 0:P],
                                               pcp[:, 4 * g:4 * g + 4, :].rearrange("p h b -> p (h b)"), ident)
                last.then_inc(pe_cT, 1)
                pe.wait_ge(cT_saved, t + 1)
                for g in range(2):
                    mm(ps[:, 6, g * S:(g + 1) * S], pcT[:, g, :],
                       vbd[:, g, :, :].rearrange("p j n -> p (j n)"), g == 0, False)

            def scores(n):
                t, k, g = GROUPS[n]
                w = width(t, k)
                if n >= 2:
                    if GROUPS[n - 2][1] == "mem":
                        pe.wait_ge(exp_done, 4 * (n - 1))
                    else:
                        pe.wait_ge(neg_ready, n - 1)
                for j in range(4):
                    q0, q1 = t * P, (t + 1) * P
                    if k in ("sel", "win"):
                        r = slice(64 * g, 64 * g + 64)
                        ops = (TT[r, NQ + j, q0:q1], TT[r, KS if k == "sel" else KW, 0:w])
                    elif k == "dsa":
                        r = slice(64 * (j % 2), 64 * (j % 2) + 64)
                        ops = (TT[r, DQ + j // 2, q0:q1], TT[r, KDD, 0:w])
                    else:
                        r = slice(64 * (j % 2), 64 * (j % 2) + 64)
                        ops = (mq[r, 0, j // 2, q0:q1], mq[r, 1, j // 2, :])
                    pl = place(j)
                    last = mm(ps[:, 2 * (n % 2) + pl // 2, (pl % 2) * S:(pl % 2) * S + w], *ops, pl % 2 == 0, True)
                last.then_inc(pe_s, 1)

            def turn(n):
                t, k, g = GROUPS[n]
                nb = width(t, k) // P
                pe.wait_ge(prob_ready, n + 1)
                if n >= 1:
                    pe.wait_ge(pT_saved, n)
                for j in range(4):
                    for b in range(nb):
                        q = j * nb + b
                        last = nc.tensor.transpose(ps[:, 4 + q // 4, (q % 4) * P:(q % 4 + 1) * P],
                                                   xb[:, n % 2, j, b * P:(b + 1) * P], ident)
                last.then_inc(pe_pT, 1)

            def outputs(n):
                t, k, g = GROUPS[n]
                nb = width(t, k) // P
                pe.wait_ge(pT_saved, n + 1)
                for j in range(4):
                    for b in range(nb):
                        if k == "sel":
                            v = h[:, b, C_VS + g * HD:C_VS + (g + 1) * HD]
                        elif k == "win":
                            v = h[:, b, C_VW + g * HD:C_VW + (g + 1) * HD]
                        elif k == "dsa":
                            v = h[:, b, C_VD:C_VD + HD]
                        else:
                            v = mq[:, 2, b, j * HD:(j + 1) * HD]
                        if k in ("sel", "win"):
                            o = ps[:, 6, (4 * g + j) * HD:(4 * g + j + 1) * HD]
                        else:
                            c0 = (0 if k == "dsa" else S) + j * HD
                            o = ps[:, 7, c0:c0 + HD]
                        last = mm(o, PT[:, n % 2, j, b * P:(b + 1) * P], v,
                                  k == "mem" and j == 0 and b == 0, True)
                last.then_inc(pe_pv, 1)

            for t in range(T):
                if t == 0:
                    cmp_scores(0)
                    pe.wait_ge(relu_done, 16)
                    scores(0)
                else:
                    pe.wait_ge(pT_saved, len(KINDS) * t)
                    cmp_scores(t)
                if t:
                    pe.wait_ge(o_saved, 2 * t)
                cmp_out(t)
                for n in range(t * len(KINDS), (t + 1) * len(KINDS)):
                    if n + 1 < len(GROUPS):
                        scores(n + 1)
                    turn(n)
                    if n % len(KINDS):
                        outputs(n - 1)
                outputs((t + 1) * len(KINDS) - 1)

            for t in range(T):
                pe.wait_ge(o_saved, 2 * t + 2)
                if t == 0:
                    pe.wait_ge(exp_done, 4 * len(GROUPS))
                for k in range(KD):
                    last = nc.tensor.transpose(ps[:, 2 * t + k // 4, (k % 4) * P:(k % 4 + 1) * P],
                                               ocs[t][:, k * P:(k + 1) * P], ident)
                last.then_inc(pe_oT, 1)
            pe.wait_ge(l_wo, 16)
            for t in range(T):
                pe.wait_ge(oT_saved, t + 1)
                for half in range(2):
                    for k in range(KD):
                        last = mm(ps[:, 4 + 2 * t + half, :], oT[:, k, t * P:(t + 1) * P],
                                  w_o[:, k, half * 512:(half + 1) * 512], k == 0, k == KD - 1)
                last.then_inc(pe_mix, 1)

            for t in range(T):
                pe.wait_ge(x1_ready, t + 1)
                for k in range(KD):
                    last = nc.tensor.transpose(ps[:, 2 * t + k // 4, (k % 4) * P:(k % 4 + 1) * P],
                                               xs[:, t, k * P:(k + 1) * P], ident)
                last.then_inc(pe_xT, 1)

            pe.wait_ge(l_wqa, 16)
            pe.wait_ge(l_sk, 16)
            pe.wait_ge(xT_saved, 2)

            def subkey_scores(b):
                pe.wait_ge(q_saved, b + 1)
                if b >= 2:
                    pe.wait_ge(sk_saved, b - 1)
                for t in range(T):
                    last = mm(ps[:, 6 + b % 2, t * P:(t + 1) * P], qT[:, b % 2, t * P:(t + 1) * P],
                              subk_sb[:, b % 2, :], t == 0, True)
                last.then_inc(pe_sk, 1)

            for b in range(2 * PH):
                if b == PH:
                    pe.wait_ge(l_wqb, 16)
                if b >= 2:
                    pe.wait_ge(q_saved, b - 1)
                for k in range(KD):
                    last = mm(ps[:, 4 + b % 2, 0:S], wq_sb[b // PH][:, k, (b % PH) * P:(b % PH + 1) * P],
                              x1T[:, k, :], k == 0, k == KD - 1)
                last.then_inc(pe_q, 1)
                if b >= 1:
                    subkey_scores(b - 1)
            subkey_scores(2 * PH - 1)

            def products(b, u_hi_, u_lo_):
                for k in range(KD):
                    ks = slice(k * P, (k + 1) * P)
                    ws = ((u_hi_[:, ks], 0), (u_hi_[:, ks], 1), (u_lo_[:, ks], 0))
                    for m, (w, part) in enumerate(ws):
                        last = mm(ps[:, b % 2, 0:S], w, x1hl[:, k, part, :], k == 0 and m == 0,
                                  k == KD - 1 and m == 2)
                return last

            def ahead(i, first):
                for b in range(RB):
                    pe.wait_ge(pu_lo, i * RB + (b + 1))
                    if not first or b >= 2:
                        pe.wait_ge(pre_gelu, i * RB + (b - 1))
                    products(b, pre(hi, b), pre(lo, b)).then_inc(pe_ph, 1)

            pe.wait_ge(x1_split, 2)
            ahead(0, True)
            with pe.Fori(1, NP) as i:
                ahead(i, False)

            for t in range(T):
                pe.wait_ge(route_ready, t + 1)
                for a in range(3):
                    last = nc.tensor.transpose(ps[:, 2 + t, a * P:(a + 1) * P], ex[:, t, a, :], ident)
                last.then_inc(pe_rT, 1)

            def gates(i, first):
                for b in range(OB):
                    pe.wait_ge(oh_ready, i * OB + (b + 1))
                    pe.wait_ge(oh2_ready, i * OB + (b + 1))
                    pe.wait_ge(oh3_ready, i * OB + (b + 1))
                    if not first:
                        pe.wait_ge(pre_gated, i * OB + (b - OB + 1))
                    for q in range(4):
                        last = mm(ps[:, gate_bank(b), q * P:(q + 1) * P], hot(b)[:, 0, q, :], hot(b)[:, 1, q, :],
                                  q == 0, True)
                    last.then_inc(pe_g, 1)

            gates(0, True)
            with pe.Fori(1, GN // OB) as i:
                gates(i, False)

            def expert_in(j, b, first):
                pe.wait_ge(u_lo, j * RB + (b + 1))
                if not first:
                    pe.wait_ge(gelu_done, j * RB + (b - 1))
                products(b, hi[:, b % 2, 0, :], lo[:, b, 0, :]).then_inc(pe_h, 1)

            def expert_out(i, b, first, final):
                pe.wait_ge(v_lo, i * RB + (b + 1))
                pe.wait_ge(a_lo, i * RB + (b + 1))
                for t in range(T):
                    vs = ((0, hi[:, b % 2, 1, :]), (0, lo[:, b % RB, 1, :]), (1, hi[:, b % 2, 1, :]))
                    for m, (part, v) in enumerate(vs):
                        for half in range(2):
                            last = mm(ps[:, 4 + 2 * t + half, :], ahl[:, b % 2, part, t * P:(t + 1) * P],
                                      v[:, half * 512:(half + 1) * 512], first and m == 0, final and m == 2)
                last.then_inc(pe_y, 1)

            pe.wait_ge(pre_gelu, NPRE)
            pe.wait_ge(pre_gated, GN)
            for b in range(RB):
                expert_out(0, b, b == 0, False)
            with pe.Fori(1, NP - 1) as i:
                for b in range(RB):
                    expert_out(i, b, False, False)
            for b in range(RB - 1):
                expert_out(NP - 1, b, False, False)
            for b in range(RB):
                expert_in(0, b, b < 2)
                expert_out(NP, b - 1, False, False)
            with pe.Fori(1, NM) as j:
                for b in range(RB):
                    expert_in(j, b, False)
                    expert_out(j + NP, b - 1, False, False)
            expert_out(NK // RB - 1, RB - 1, False, True)

        @block.scalar
        def _(act):
            act.wait_ge(ang_ready, 1)
            nc.scalar.activation(sinv, turns, ACT.Sin).then_inc(trig, 1)
            nc.scalar.activation(cosv, ang, ACT.Sin).then_inc(trig, 1)
            for t in range(T):
                for n, (c0, w) in enumerate(CHUNKS):
                    act.wait_ge(pe_proj, t * 4 + n + 1)
                    nc.scalar.copy(h[:, t, c0:c0 + w], ps[:, t * 4 + n, 0:w]).then_inc(h_saved, 1)
                nc.scalar.activation(gate[:, t, :, :].rearrange("p h b -> p (h b)"),
                                     ps[:, t * 4 + 3, C_GATE - 1536:C_GATE - 1536 + 24], ACT.Exp, scale=-1.0
                                     ).then_inc(gate_exp, 1)
            for m in range(6):
                act.wait_ge(pe_memp, m + 1)
                nc.scalar.copy(mq[:, m // 2, m % 2, :], ps[:, m, 0:S]).then_inc(mem_saved, 1)

            for t in range(T):
                for q in range(4):
                    act.wait_ge(pe_tr, t * 4 + q + 1)
                    v = ps[:, t * 4 + q, :].rearrange("p (s n) -> p s n", s=4)
                    if q < 3:
                        nc.scalar.copy(TT[:, 4 * q:4 * q + 4, t * P:(t + 1) * P], v).then_inc(tr_saved, 1)
                    else:
                        nc.scalar.copy(TT[0:64, 12:16, t * P:(t + 1) * P], v[0:64])
                        if t == 0:
                            nc.scalar.copy(TT[64:128, 12:16, 0:P - 1], v[64:128, :, 1:P]).then_inc(tr_saved, 1)
                        else:
                            nc.scalar.copy(TT[64:128, 12:16, P - 1:2 * P - 1], v[64:128]).then_inc(tr_saved, 1)

            act.wait_ge(pad_zero, 1)
            act.wait_ge(pe_hid, 1)
            nc.scalar.activation(ghk[:, 0:2 * NC], ps[:, 0, 0:2 * NC], ACT.Gelu).then_inc(hid_act, 1)
            act.wait_ge(pe_hid, 2)
            for g in range(2):
                nc.scalar.activation(ghv[:, g, :, 0:NC],
                                     ps[:, 1, g * NC:(g + 1) * NC].unsqueeze(1).to_broadcast([P, 4, NC]),
                                     ACT.Gelu).then_inc(hid_act, 1)

            for t in range(T):
                w = width(t, "idx")
                act.wait_ge(pe_idx, t + 1)
                if t:
                    act.wait_ge(idx_read, 8)
                for i in range(IDX_H):
                    nc.scalar.activation(rl[:, i // 4, i % 4, 0:w],
                                         ps[:, i % 4, (i // 4) * S:(i // 4) * S + w], ACT.Relu).then_inc(relu_done, 1)

            def cmp_exp(t):
                act.wait_ge(cx_ready, t + 1)
                nc.scalar.activation(pc, pc, ACT.Exp, scale=SCALE).then_inc(cx_exp, 1)

            def save_o(t):
                act.wait_ge(pe_pv, (t + 1) * len(KINDS))
                for half in range(2):
                    nc.scalar.copy(ocs[t][:, half * 512:(half + 1) * 512], ps[:, 6 + half, :]).then_inc(o_saved, 1)

            act.wait_ge(idx_read, 16)
            for n, (t, k, g) in enumerate(GROUPS):
                w = width(t, k)
                if n % len(KINDS) == 0:
                    cmp_exp(t)
                act.wait_ge(neg_ready, n + 1)
                for j in range(4):
                    c = 4 * (n % 2) + j
                    pl = place(j)
                    src = (ps[:, 2 * (n % 2) + pl // 2, (pl % 2) * S:(pl % 2) * S + w] if k == "mem"
                           else xb[:, n % 2, j, 0:w])
                    nc.scalar.activation(xb[:, n % 2, j, 0:w], src, ACT.Exp, bias=gneg[:, c:c + 1], scale=SCALE,
                                         accum_out=gden[:, c:c + 1]).then_inc(exp_done, 1)
                if n % len(KINDS) == 0:
                    act.wait_ge(pe_cT, t + 1)
                    nc.scalar.copy(pcT, ps[:, 4:6, 0:P]).then_inc(cT_saved, 1)
                act.wait_ge(pe_pT, n + 1)
                if n >= 2:
                    act.wait_ge(pe_pv, n - 1)
                nc.scalar.copy(PT[:, n % 2, :, 0:w],
                               bank2(2)[:, 0:4 * w].rearrange("p (j n) -> p j n", j=4)).then_inc(pT_saved, 1)
                if n % len(KINDS) == len(KINDS) - 1:
                    save_o(t)

            for t in range(T):
                act.wait_ge(pe_oT, t + 1)
                nc.scalar.copy(oT[:, :, t * P:(t + 1) * P],
                               bank2(t).rearrange("p (k n) -> p k n", k=KD)).then_inc(oT_saved, 1)

            def norm(n, tiles):
                for t in tiles:
                    act.wait_ge(centred, n * T + t + 1)
                    nc.scalar.activation(junk[:, t, :], xs[:, t, :], ACT.Square,
                                         accum_out=lnst[:, t, 2:3]).then_inc(squared, 1)
                for t in tiles:
                    act.wait_ge(var_ready, n * T + t + 1)
                    nc.scalar.activation(lnst[:, t, 4:5], lnst[:, t, 3:4], ACT.Sqrt).then_inc(rooted, 1)

            for t in range(T):
                norm(0, [t])
            for t in range(T):
                act.wait_ge(pe_xT, t + 1)
                nc.scalar.copy(x1T[:, :, t * P:(t + 1) * P],
                               bank2(t).rearrange("p (k n) -> p k n", k=KD)).then_inc(xT_saved, 1)

            def save_scores(b):
                act.wait_ge(pe_sk, b + 1)
                nc.scalar.copy(sc[:, :, b, :], ps[:, 6 + b % 2, 0:S].rearrange("p (t n) -> p t n", t=T)
                               ).then_inc(sk_saved, 1)

            for b in range(2 * PH):
                act.wait_ge(pe_q, b + 1)
                if b >= 2:
                    act.wait_ge(pe_sk, b - 1)
                nc.scalar.copy(qT[:, b % 2, :], ps[:, 4 + b % 2, 0:S]).then_inc(q_saved, 1)
                if b >= 1:
                    save_scores(b - 1)
            save_scores(2 * PH - 1)

            def split_pre(i, b, first):
                act.wait_ge(pu_in[b], (i + 1) * 16)
                if not first:
                    act.wait_ge(pe_ph, i * RB + (b - RB + 1))
                nc.scalar.copy(pre(hi, b), pre(raw, b)).then_inc(pu_hi, 1)

            def gelu_pre(i, b):
                act.wait_ge(pe_ph, i * RB + (b + 1))
                nc.scalar.activation(G[:, bass.ds(i * RB + b, 1), :].rearrange("p o t -> p (o t)"),
                                     ps[:, b % 2, 0:S], ACT.Gelu).then_inc(pre_gelu, 1)

            for b in range(RB):
                split_pre(0, b, True)
                if b >= 2:
                    gelu_pre(0, b - 2)
            with act.Fori(1, NP) as i:
                for b in range(RB):
                    split_pre(i, b, False)
                    gelu_pre(i, b - 2)
            gelu_pre(NP - 1, RB - 2)
            gelu_pre(NP - 1, RB - 1)

            for t in range(T):
                act.wait_ge(g_shift, t + 1)
                nc.scalar.activation(te[:, t], te[:, t], ACT.Exp).then_inc(g_exp, 1)
            for t in range(T):
                act.wait_ge(pe_rT, t + 1)
                nc.scalar.copy(slotT[:, :, t * P:(t + 1) * P],
                               ps[:, 2 + t, 0:3 * P].rearrange("p (a n) -> p a n", a=3)).then_inc(rT_saved, 1)

            def onehot(i, b, first):
                nc.scalar.activation(gel[:, b % 2, 0:P], iota, ACT.Abs, scale=-1.0,
                                     bias=slotT[:, 1, bass.ds(i * (4 * OB) + (b * 4 + POOL_HOT), 1)]
                                     ).then_inc(hot_dist, 1)
                if not first:
                    act.wait_ge(pe_g, i * OB + (b - OB + 1))
                act.wait_ge(hot_dist, i * OB + (b + 1))
                nc.scalar.activation(hot(b)[:, 0, POOL_HOT, :], gel[:, b % 2, 0:P], ACT.Relu, scale=-1.0, bias=1.0
                                     ).then_inc(oh3_ready, 1)

            def save_gates(i, b):
                act.wait_ge(pe_g, i * OB + (b + 1))
                nc.scalar.copy(G[:, NPRE:NK, bass.ds(i * (4 * OB) + b * 4, 4)].rearrange("p c q -> p q c"),
                               ps[:, gate_bank(b % OB), :].rearrange("p (q c) -> p q c", q=4)[:, :, NPRE:NK]
                               ).then_inc(g_saved, 1)

            act.wait_ge(rT_saved, T)
            for b in range(OB):
                onehot(0, b, True)
                if b:
                    save_gates(0, b - 1)
            with act.Fori(1, GN // OB) as i:
                for b in range(OB):
                    onehot(i, b, False)
                    save_gates(i, b - 1)
            save_gates(GN // OB - 1, OB - 1)

            def u_split(j, b, first):
                act.wait_ge(u_in[b], (j + 1) * 16)
                if not first:
                    act.wait_ge(pe_h, j * RB + (b - 1))
                nc.scalar.copy(hi[:, b % 2, 0, :], raw[:, b, 0, :]).then_inc(u_hi, 1)

            def v_split(i, b, first):
                act.wait_ge(v_in[b], (i + 1) * 16)
                if not first:
                    act.wait_ge(pe_y, i * RB + (b - 1))
                nc.scalar.copy(hi[:, b % 2, 1, :], raw[:, b, 1, :]).then_inc(v_hi, 1)

            def gelu(j, b, first):
                act.wait_ge(pe_h, j * RB + (b + 1))
                if not first:
                    act.wait_ge(a_lo, j * RB + (NPRE + b - 1))
                nc.scalar.activation(gel[:, b % 2, :], ps[:, b % 2, 0:S], ACT.Gelu).then_inc(gelu_done, 1)

            for b in range(RB):
                v_split(0, b, b < 2)
            with act.Fori(1, NP) as i:
                for b in range(RB):
                    v_split(i, b, False)
            for b in range(RB):
                u_split(0, b, b < 2)
                if b:
                    gelu(0, b - 1, b - 1 < 2)
                v_split(NP, b, False)
            with act.Fori(1, NM) as j:
                for b in range(RB):
                    u_split(j, b, False)
                    gelu(j, b - 1, False)
                    v_split(j + NP, b, False)
            gelu(NM - 1, RB - 1, False)
            norm(1, range(T))

        @block.vector
        def _(dve):
            v = nc.vector
            count = [0]

            def did(ins):
                count[0] += 1
                ins.then_inc(dve_chain, 1)

            def settle():
                dve.wait_ge(dve_chain, count[0])

            dve.wait_ge(l_const, 16)
            dve.wait_ge(l_pos, 16)
            did(v.tensor_copy(posf, pos_i[:, :]))
            settle()
            for t in range(T):
                did(v.tensor_scalar(ang[:, t, :], kc[:, K_FREQ:K_FREQ + 12], posf[:, t:t + 1], None, ALU.mult))
            settle()
            did(v.tensor_scalar(turns, ang, 1.0 / (2 * np.pi), MAGIC, ALU.mult, ALU.add))
            settle()
            did(v.tensor_scalar(turns, turns, -MAGIC, None, ALU.add))
            settle()
            for part in TWO_PI:
                did(v.scalar_tensor_tensor(out=ang, in0=turns, scalar=-part, in1=ang, op0=ALU.mult, op1=ALU.add))
                settle()
            did(v.tensor_scalar(turns, ang, PI_IN, -PI_IN, ALU.min, ALU.max))
            did(v.tensor_scalar(sinv, ang, float(np.float32(np.pi / 2)), None, ALU.is_gt))
            settle()
            did(v.tensor_scalar(ang, ang, float(np.float32(np.pi / 2)), None, ALU.add))
            settle()
            did(v.scalar_tensor_tensor(out=ang, in0=sinv, scalar=float(np.float32(-2 * np.pi)), in1=ang,
                                       op0=ALU.mult, op1=ALU.add))
            settle()
            did(v.tensor_scalar(ang, ang, PI_IN, -PI_IN, ALU.min, ALU.max))
            settle()
            v.tensor_scalar(turns, turns, 0.0, None, ALU.add).then_inc(ang_ready, 1)

            dve.wait_ge(trig, 2)
            for t in range(T):
                dve.wait_ge(h_saved, 4 * (t + 1))
                jobs = []
                for c0, heads, hd, f0, r0 in ((0, N64, HD, 0, 0), (C_IQ, N32, IDX_D, 8, 608)):
                    half = hd // 8
                    hv = h[:, t, c0:c0 + heads * hd].rearrange("p (h d) -> p h d", h=heads)
                    x1, x2 = hv[:, :, 0:half], hv[:, :, half:2 * half]
                    cs = cosv[:, t, f0:f0 + half].unsqueeze(1).to_broadcast([P, heads, half])
                    sn = sinv[:, t, f0:f0 + half].unsqueeze(1).to_broadcast([P, heads, half])
                    n = heads * half
                    tmp = [rt[:, r0 + m * n:r0 + (m + 1) * n].rearrange("p (h d) -> p h d", h=heads)
                           for m in range(4)]
                    did(v.tensor_tensor(tmp[0], x1, cs, ALU.mult))
                    did(v.tensor_tensor(tmp[1], x2, sn, ALU.mult))
                    did(v.tensor_tensor(tmp[2], x2, cs, ALU.mult))
                    did(v.tensor_tensor(tmp[3], x1, sn, ALU.mult))
                    jobs.append((x1, x2, tmp))
                settle()
                for x1, x2, tmp in jobs:
                    did(v.tensor_tensor(x1, tmp[0], tmp[1], ALU.subtract))
                    did(v.tensor_tensor(x2, tmp[2], tmp[3], ALU.add))
                settle()
                for d0, c0, g, n, w in ((0, C_KD, 1, 2, HD), (128, C_IK, 1, 4, IDX_D), (256, C_KC, 2, 2, HD),
                                        (512, C_VC, 2, 2, HD)):
                    for gg in range(g):
                        o = dup[:, t, d0 + gg * n * w:d0 + (gg + 1) * n * w].rearrange("p (n w) -> p n w", n=n)
                        did(v.tensor_copy(o, h[:, t, c0 + gg * w:c0 + (gg + 1) * w].unsqueeze(1)
                                          .to_broadcast([P, n, w])))
                did(v.tensor_scalar(iw[:, t, :], h[:, t, C_IW:C_IW + IDX_H], (IDX_H * IDX_D) ** -0.5, None, ALU.mult))
                settle()
                v.tensor_scalar(iw[:, t, :], iw[:, t, :], 0.0, None, ALU.add).then_inc(roped, 1)
                dve.wait_ge(gate_exp, t + 1)
                gt = gate[:, t, :, :].rearrange("p h b -> p (h b)")
                did(v.tensor_scalar(gt, gt, 1.0, None, ALU.add))
                settle()
                did(v.reciprocal(gt, gt))

            dve.wait_ge(pe_memp, 2)
            did(v.memset(ghv, 0.0))
            did(v.memset(vbd, 0.0))
            did(v.memset(pcp, 0.0))
            settle()
            v.memset(ghk, 0.0).then_inc(pad_zero, 1)

            dve.wait_ge(l_pe, 16)
            dve.wait_ge(tr_saved, 8)
            for a in range(2):
                s0 = KC if a == 0 else VC
                for g in range(2):
                    src = bass.AP(TT.tensor, TT[:, s0 + g, :].offset, [list(TT.ap[0]), [2, LP], [CMP_STRIDE, NC]])
                    ins = v.tensor_tensor(flat[:, a, :, g, :], src,
                                          pe_sb[:, a, :].unsqueeze(2).to_broadcast([P, LP, NC]), ALU.add)
                ins.then_inc(flat_ready, 1)

            dve.wait_ge(pe_kv, 1)
            did(v.tensor_copy(kcT[0:64, 0:NC], ps[0:64, 2, 0:NC]))
            v.tensor_copy(kcT[64:128, 0:NC], ps[64:128, 2, NC:2 * NC]).then_inc(kv_saved, 1)
            dve.wait_ge(pe_kv, 3)
            for g in range(2):
                for j in range(4):
                    r = slice(32 * j, 32 * j + 32)
                    ins = v.tensor_copy(vbd[r, g, j, :], ps[r, 3 + g, 0:HD])
                ins.then_inc(kv_saved, 1)

            for t in range(T):
                w = width(t, "idx")
                tri = kc[:, K_TRI + S - w:K_TRI + S]
                for i in range(IDX_H):
                    dve.wait_ge(relu_done, 8 * t + i + 1)
                    if i:
                        dve.wait_ge(idx_read, 8 * t + i)
                    v.scalar_tensor_tensor(out=score[:, t, 0:w], in0=rl[:, i // 4, i % 4, 0:w],
                                           scalar=iw[:, t, i:i + 1], in1=tri if i == 0 else score[:, t, 0:w],
                                           op0=ALU.mult, op1=ALU.add).then_inc(idx_read, 1)

            def index_round(t):
                w = width(t, "idx")
                did(v.max(top8, score[:, t, 0:w]))
                settle()
                did(v.match_replace(score[:, t, 0:w], top8, score[:, t, 0:w], TAKEN))
                settle()

            def index_bias(t):
                w = width(t, "idx")
                did(v.tensor_scalar(dbias[:, t, 0:w], score[:, t, 0:w], TAKEN, NEG, ALU.not_equal, ALU.mult))
                settle()
                did(v.tensor_tensor(dbias[:, t, 0:w], dbias[:, t, 0:w], kc[:, K_TRI + S - w:K_TRI + S], ALU.add))
                settle()

            def cmp_scores(t):
                dve.wait_ge(pe_cs, t + 1)
                if t:
                    dve.wait_ge(pe_cT, t)
                cb = kc[:, K_CB + t * NC:K_CB + (t + 1) * NC].unsqueeze(1).to_broadcast([P, 4, NC])
                for g in range(2):
                    did(v.tensor_tensor(pc[:, 4 * g:4 * g + 4, :],
                                        ps[:, 4 + g, 0:64].rearrange("p (j b) -> p j b", j=4)[:, :, 0:NC],
                                        cb, ALU.add))
                settle()
                did(v.tensor_reduce(cmax, pc, AX_X, ALU.max))
                settle()
                did(v.tensor_scalar(cmax, cmax, NEG / 10, None, ALU.max))
                settle()
                v.tensor_tensor(pc, pc, cmax.unsqueeze(2).to_broadcast([P, 8, NC]), ALU.subtract
                                ).then_inc(cx_ready, 1)

            def cmp_probs(t):
                dve.wait_ge(cx_exp, t + 1)
                did(v.tensor_reduce(cmax, pc, AX_X, ALU.add))
                settle()
                did(v.tensor_scalar(cmax, cmax, 1e-30, None, ALU.max))
                settle()
                did(v.reciprocal(cmax, cmax))
                settle()
                did(v.tensor_tensor(cmax, cmax, gate[:, t, :, 0], ALU.mult))
                settle()
                v.tensor_tensor(pcp[:, :, 0:NC], pc, cmax.unsqueeze(2).to_broadcast([P, 8, NC]), ALU.mult
                                ).then_inc(cp_ready, 1)

            def maxima(n):
                t, k, g = GROUPS[n]
                w = width(t, k)
                dve.wait_ge(pe_s, n + 1)
                if n >= 2:
                    dve.wait_ge(pe_pT, n - 1)
                for j in range(4):
                    pl = place(j)
                    c = 4 * (n % 2) + j
                    s = ps[:, 2 * (n % 2) + pl // 2, (pl % 2) * S:(pl % 2) * S + w]
                    if k == "mem":
                        did(v.tensor_reduce(gmax[:, c:c + 1], s, AX_X, ALU.max))
                    else:
                        bias = dbias[:, t, 0:w] if k == "dsa" else kc[:, K_TRI + S - w:K_TRI + S]
                        did(v.tensor_tensor_reduce(out=xb[:, n % 2, j, 0:w], in0=s, in1=bias, scale=1.0,
                                                   scalar=TAKEN, op0=ALU.add, op1=ALU.max,
                                                   accum_out=gmax[:, c:c + 1]))
                settle()
                c = slice(4 * (n % 2), 4 * (n % 2) + 4)
                v.tensor_scalar(gneg[:, c], gmax[:, c], -SCALE, None, ALU.mult).then_inc(neg_ready, 1)

            def normalise(n):
                t, k, g = GROUPS[n]
                w = width(t, k)
                c = slice(4 * (n % 2), 4 * (n % 2) + 4)
                dve.wait_ge(exp_done, 4 * (n + 1))
                did(v.reciprocal(grec[:, c], gden[:, c]))
                settle()
                if k in ("sel", "win"):
                    did(v.tensor_tensor(grec[:, c], grec[:, c],
                                        gate[:, t, 4 * g:4 * g + 4, 1 if k == "sel" else 2], ALU.mult))
                    settle()
                for j in range(4):
                    ins = v.tensor_scalar(xb[:, n % 2, j, 0:w], xb[:, n % 2, j, 0:w],
                                          grec[:, 4 * (n % 2) + j:4 * (n % 2) + j + 1], None, ALU.mult)
                ins.then_inc(prob_ready, 1)

            for t in range(T):
                n0 = t * len(KINDS)
                cmp_scores(t)
                if t == 0:
                    maxima(0)
                cmp_probs(t)
                dve.wait_ge(idx_read, 8 * (t + 1))
                for n in range(n0, n0 + len(KINDS)):
                    normalise(n)
                    if n + 1 < len(GROUPS):
                        maxima(n + 1)
                    if n < n0 + 4:
                        for _ in range(TOPK_DSA // 8 // 4):
                            index_round(t)
                    if n == n0 + 3:
                        index_bias(t)

            def norm(n, tiles, param):
                for t in tiles:
                    did(v.scalar_tensor_tensor(out=xs[:, t, :], in0=xs[:, t, :], scalar=ALPHA, in1=bank2(2 + t),
                                               op0=ALU.mult, op1=ALU.add, accum_out=lnst[:, t, 0:1]))
                    settle()
                    did(v.tensor_scalar(lnst[:, t, 1:2], lnst[:, t, 0:1], 1.0 / D, None, ALU.mult))
                    settle()
                    v.tensor_scalar(xs[:, t, :], xs[:, t, :], lnst[:, t, 1:2], None, ALU.subtract
                                    ).then_inc(centred, 1)
                for t in tiles:
                    dve.wait_ge(squared, n * T + t + 1)
                    v.tensor_scalar(lnst[:, t, 3:4], lnst[:, t, 2:3], 1.0 / D, EPS, ALU.mult, ALU.add
                                    ).then_inc(var_ready, 1)
                for t in tiles:
                    dve.wait_ge(rooted, n * T + t + 1)
                    did(v.reciprocal(lnst[:, t, 5:6], lnst[:, t, 4:5]))
                    settle()
                    did(v.scalar_tensor_tensor(out=xs[:, t, :], in0=xs[:, t, :], scalar=lnst[:, t, 5:6],
                                               in1=param[:, 0, :], op0=ALU.mult, op1=ALU.mult))
                    settle()
                    v.tensor_tensor(xs[:, t, :], xs[:, t, :], param[:, 1, :], ALU.add
                                    ).then_inc(x1_ready if n == 0 else y_ready, 1)

            dve.wait_ge(l_x, 16)
            dve.wait_ge(l_ln1, 16)
            for t in range(T):
                dve.wait_ge(pe_mix, t + 1)
                norm(0, [t], ln_sb)

            dve.wait_ge(xT_saved, T)
            v.tensor_copy(x1hl[:, :, 0, :], x1T).then_inc(x1_split, 1)
            dve.wait_ge(x1_split, 1)
            v.tensor_tensor(x1hl[:, :, 1, :], x1T, x1hl[:, :, 0, :].bitcast(F32), ALU.subtract).then_inc(x1_split, 1)

            def top16(jobs):
                for o in (0, 8):
                    for vals, _, s in jobs:
                        did(v.max(vals[:, o:o + 8], s))
                    settle()
                    for vals, idx, s in jobs:
                        did(v.max_index(idx[:, o:o + 8], vals[:, o:o + 8], s))
                    if o == 0:
                        settle()
                        for vals, _, s in jobs:
                            did(v.match_replace(s, vals[:, 0:8], s, TAKEN))
                    settle()

            for b in range(2 * PH):
                dve.wait_ge(sk_saved, b + 1)
                top16([(V[:, t, b, :], IX[:, t, b, :], sc[:, t, b, :]) for t in range(T)])

            for t in range(T):
                did(v.tensor_copy(IF, IX[:, t, :, :]))
                settle()
                i1 = IF.rearrange("p (h a) k -> p h a k", a=2)[:, :, 0, :]
                i2 = IF.rearrange("p (h a) k -> p h a k", a=2)[:, :, 1, :]
                v1 = V[:, t, :, :].rearrange("p (h a) k -> p h a k", a=2)[:, :, 0, :]
                v2 = V[:, t, :, :].rearrange("p (h a) k -> p h a k", a=2)[:, :, 1, :]
                did(v.tensor_scalar(i1, i1, float(NK), None, ALU.mult))
                settle()
                for r0, r, c in RUNS:
                    sl = slice(OFF[r0], OFF[r0] + r * c)
                    for o, a1, a2 in ((cand, v1, v2), (cande, i1, i2)):
                        did(v.tensor_tensor(o[:, :, sl].rearrange("p h (r c) -> p h r c", r=r),
                                            a1[:, :, r0:r0 + r].unsqueeze(3).to_broadcast([P, PH, r, c]),
                                            a2[:, :, 0:c].unsqueeze(2).to_broadcast([P, PH, r, c]), ALU.add))
                settle()
                top16([(tv[:, hh, :], ti[:, hh, :], cand[:, hh, :]) for hh in range(PH)])
                v.tensor_tensor(te[:, t], tv, tv[:, :, 0:1].to_broadcast([P, PH, TK]), ALU.subtract).then_inc(g_shift, 1)
                did(v.tensor_copy(tf, ti))
                settle()
                eqv = eq.rearrange("p (m c) -> p m c", c=NCAND)
                did(v.tensor_tensor(eqv, tf.rearrange("p h k -> p (h k)").unsqueeze(2).to_broadcast([P, PH * TK, NCAND]),
                                    kc[:, K_IOTA:K_IOTA + NCAND].unsqueeze(1).to_broadcast([P, PH * TK, NCAND]),
                                    ALU.is_equal))
                settle()
                eqh = eq.rearrange("p (h k c) -> p h k c", h=PH, k=TK)
                did(v.tensor_tensor(eqh, eqh, cande.unsqueeze(2).to_broadcast([P, PH, TK, NCAND]), ALU.mult))
                settle()
                tfl = tf.rearrange("p h k -> p (h k)")
                did(v.tensor_reduce(tfl, eqv, AX_X, ALU.add))
                settle()
                did(v.tensor_scalar(ex[:, t, 0, :], tfl, 1.0 / NK, -(NK - 1) / (2.0 * NK), ALU.mult, ALU.add))
                settle()
                did(v.tensor_scalar(ex[:, t, 0, :], ex[:, t, 0, :], MAGIC, None, ALU.add))
                settle()
                did(v.tensor_scalar(ex[:, t, 0, :], ex[:, t, 0, :], -MAGIC, None, ALU.add))
                settle()
                did(v.scalar_tensor_tensor(out=ex[:, t, 1, :], in0=ex[:, t, 0, :], scalar=-float(NK), in1=tfl,
                                           op0=ALU.mult, op1=ALU.add))
            settle()
            for t in range(T):
                dve.wait_ge(g_exp, t + 1)
                did(v.tensor_reduce(gs[:, 0:PH], te[:, t], AX_X, ALU.add))
                settle()
                did(v.reciprocal(gs[:, PH:2 * PH], gs[:, 0:PH]))
                settle()
                v.tensor_tensor(ex[:, t, 2, :].rearrange("p (h k) -> p h k", h=PH), te[:, t],
                                gs[:, PH:2 * PH].unsqueeze(2).to_broadcast([P, PH, TK]), ALU.mult
                                ).then_inc(route_ready, 1)

            def gate_ahead(i, b):
                dve.wait_ge(g_saved, i * OB + (b + 1))
                g = G[:, 0:NPRE, bass.ds(i * (4 * OB) + b * 4, 4)]
                v.tensor_tensor(g, ps[:, gate_bank(b % OB), :].rearrange("p (q c) -> p c q", q=4)[:, 0:NPRE, :], g, ALU.mult
                                ).then_inc(pre_gated, 1)

            def onehots(i, first):
                for b in range(OB):
                    if not first:
                        dve.wait_ge(pe_g, i * OB + (b - OB + 1))
                    for q in range(4):
                        tok = bass.ds(i * (4 * OB) + (b * 4 + q), 1)
                        if q > POOL_HOT:
                            v.tensor_scalar(hot(b)[:, 0, q, :], iota, slotT[:, 1, tok], None, ALU.is_equal)
                        ins = v.tensor_scalar(hot(b)[:, 1, q, :], iota, slotT[:, 0, tok], slotT[:, 2, tok],
                                              ALU.is_equal, ALU.mult)
                    ins.then_inc(oh_ready, 1)
                    if not (first and b < 2):
                        gate_ahead(i, b - 2)

            dve.wait_ge(rT_saved, T)
            onehots(0, True)
            with dve.Fori(1, GN // OB) as i:
                onehots(i, False)
            gate_ahead(GN // OB - 1, OB - 2)
            gate_ahead(GN // OB - 1, OB - 1)

            def u_rest(j, b):
                dve.wait_ge(u_hi, j * RB + (b + 1))
                v.tensor_tensor(lo[:, b, 0, :], raw[:, b, 0, :], hi[:, b % 2, 0, :].bitcast(F32),
                                ALU.subtract).then_inc(u_lo, 1)

            def v_rest(i, b):
                dve.wait_ge(v_hi, i * RB + (b + 1))
                v.tensor_tensor(lo[:, b, 1, :], raw[:, b, 1, :], hi[:, b % 2, 1, :].bitcast(F32),
                                ALU.subtract).then_inc(v_lo, 1)

            def split(i, b, a):
                v.tensor_copy(ahl[:, b % 2, 0, :], a).then_inc(a_hi, 1)
                dve.wait_ge(a_hi, i * RB + (b + 1))
                v.tensor_tensor(ahl[:, b % 2, 1, :], a, ahl[:, b % 2, 0, :].bitcast(F32),
                                ALU.subtract).then_inc(a_lo, 1)

            def a_split_pre(i, b, first):
                if not first:
                    dve.wait_ge(pe_y, i * RB + (b - 1))
                split(i, b, G[:, bass.ds(i * RB + b, 1), :].rearrange("p o t -> p (o t)"))

            def a_split(j, b):
                dve.wait_ge(gated, j * RB + (b + 1))
                dve.wait_ge(pe_y, j * RB + (NPRE + b - 1))
                split(j + NP, b, gel[:, b % 2, :])

            dve.wait_ge(pre_gated, GN)
            for b in range(RB):
                a_split_pre(0, b, b < 2)
                v_rest(0, b)
            with dve.Fori(1, NP) as i:
                for b in range(RB):
                    a_split_pre(i, b, False)
                    v_rest(i, b)
            for b in range(RB):
                u_rest(0, b)
                if b:
                    a_split(0, b - 1)
                v_rest(NP, b)
            with dve.Fori(1, NM) as j:
                for b in range(RB):
                    u_rest(j, b)
                    a_split(j, b - 1)
                    v_rest(j + NP, b)
            a_split(NM - 1, RB - 1)

            dve.wait_ge(l_ln2, 16)
            dve.wait_ge(pe_y, NK)
            norm(1, range(T), ln2_sb)


def kernel(**inputs):
    import concourse.bacc as _bacc
    from concourse.bass_utils import run_bass_kernel_spmd as _run

    a = {k: np.ascontiguousarray(v) for k, v in inputs.items()}

    def rows(w):
        return np.ascontiguousarray(w.reshape(-1, P, w.shape[-1]).transpose(1, 0, 2))

    w = a["w_in"][0]
    ends = np.cumsum([512, 768, 24, 256, 128, 256, 32, 8, 256])
    nq, kv, gt, dq, dkv, iq, ik, iwt, mqw = np.split(w, ends[:-1], axis=1)
    nq = nq.reshape(D, 2, 4, HD).transpose(0, 2, 1, 3).reshape(D, 512)
    kv = kv.reshape(D, 6, 128)
    tok = np.concatenate([nq, kv[:, 0], kv[:, 2], kv[:, 4], dq, dkv[:, :HD], iq, ik,
                          kv[:, 1], kv[:, 3], kv[:, 5], dkv[:, HD:], gt, iwt], axis=1)
    wm = a["w_mem_kv"][0]
    wq = a["peer_w_query"][0]
    w2k = a["nsa_cmp_w2_k"][0]

    def pe_rows(m):
        return m.reshape(LP, P).T

    arrays = {
        "x": rows(a["x"][0]), "xT": rows(a["x"][0].T), "memT": rows(a["mem"][0].T),
        "positions": np.ascontiguousarray(a["positions"][0].reshape(T, P).T),
        "w_tok": rows(tok), "w_memq": rows(mqw), "w_memk": rows(wm[:, :256]), "w_memv": rows(wm[:, 256:]),
        "w1k": rows(a["nsa_cmp_w1_k"][0]), "w1v": rows(a["nsa_cmp_w1_v"][0]),
        "w2k": np.concatenate([w2k, w2k], axis=1), "w2v": a["nsa_cmp_w2_v"][0],
        "peT": np.ascontiguousarray(np.stack([pe_rows(a["nsa_pe_k"][0]), pe_rows(a["nsa_pe_v"][0])], axis=1)),
        "w_out": rows(a["w_out"][0]), "ln1": np.stack([a["ln1_g"][0], a["ln1_b"][0]]),
        "wqa": rows(wq[:, :1024]), "wqb": rows(wq[:, 1024:]),
        "subk": np.ascontiguousarray(np.stack([a["peer_sub_keys_1"][0].T, a["peer_sub_keys_2"][0].T], axis=1)),
        "uT": np.ascontiguousarray(a["peer_u"][0].reshape(NK, P, KD, P).transpose(0, 3, 2, 1)).reshape(NK, P, D),
        "pv": a["peer_v"][0].reshape(NK, P, D),
        "ln2": np.stack([a["ln2_g"][0], a["ln2_b"][0]]),
        "consts": constants(),
    }
    nc = _bacc.Bacc("TRN2", target_bir_lowering=False, num_devices=1)
    args = {n: nc.dram_tensor(f"in_{n}", list(v.shape), mybir.dt.from_np(v.dtype), kind="ExternalInput").ap()
            for n, v in arrays.items()}
    out = nc.dram_tensor("out", [S, D], F32, kind="ExternalOutput").ap()
    peer_layer_kernel(nc, out=out, **args)
    r = _run(nc, [{f"in_{n}": np.ascontiguousarray(v) for n, v in arrays.items()}], core_ids=[0])
    return r.results[0]["out"].reshape(1, S, D)
```
